# Optimizing a Trainium2 kernel written in Bass

```python
import jax, jax.numpy as jnp
from jax import lax
import numpy as np

D_MODEL = 1024
BATCH = 1
SEQ = 256
DEPTH = 2

N_RET_HEADS = 4
RET_QK_DIM = 256
RET_V_DIM = 512
RET_CHUNK = 128
N_ATT_HEADS = 8
ATT_HEAD_DIM = 128
N_IDX_HEADS = 8
IDX_DIM = 64
TOPK_MAX = 256
Q_BLOCK = 128
N_GROUPS = 4
EXPERTS_PER_GROUP = 8
N_EXPERTS = N_GROUPS * EXPERTS_PER_GROUP
TOP_K_EXPERTS = 2
EXPERT_FF = 512
DISPATCH_BLOCK = 128
ROPE_THETA = 10000.0
LN_EPS = 1e-5
GN_EPS = 1e-5
DEEPNORM_ALPHA = (2 * DEPTH) ** 0.25
DEEPNORM_BETA = (8 * DEPTH) ** -0.25

RET_Q_W = N_RET_HEADS * RET_QK_DIM
RET_V_W = N_RET_HEADS * RET_V_DIM
ATT_Q_W = N_ATT_HEADS * ATT_HEAD_DIM
IDX_Q_W = N_IDX_HEADS * IDX_DIM
COL_SIZES = (RET_Q_W, RET_Q_W, RET_V_W, RET_V_W, ATT_Q_W, ATT_HEAD_DIM, ATT_HEAD_DIM,
             IDX_Q_W, IDX_DIM, N_IDX_HEADS, D_MODEL, D_MODEL)
IN_WIDTH = sum(COL_SIZES)

kernel_name = 'hybrid_retention_dsa_hiermoe_deepnorm'

def layer_norm(x, g, b):
    xf = x.astype(jnp.float32)
    mu = xf.mean(-1, keepdims=True)
    var = jnp.square(xf - mu).mean(-1, keepdims=True)
    y = (xf - mu) * lax.rsqrt(var + LN_EPS)
    return (y * g.astype(jnp.float32) + b.astype(jnp.float32)).astype(x.dtype)

def rotary(x, pos):
    d = x.shape[-1]
    inv = 1.0 / (ROPE_THETA ** (jnp.arange(0, d, 2, dtype=jnp.float32) / d))
    ang = pos.astype(jnp.float32)[:, None] * inv[None, :]
    cos = jnp.cos(ang)[None, :, None, :].astype(x.dtype)
    sin = jnp.sin(ang)[None, :, None, :].astype(x.dtype)
    x1, x2 = x[..., : d // 2], x[..., d // 2:]
    return jnp.concatenate([x1 * cos - x2 * sin, x2 * cos + x1 * sin], axis=-1)

def retention(q, k, v, g):
    B, S, H, dk = q.shape
    dv = v.shape[-1]
    C = RET_CHUNK
    N = S // C
    log_gamma = jnp.log(1.0 - 2.0 ** (-5.0 - jnp.arange(H, dtype=jnp.float32)))
    pos = jnp.arange(C, dtype=jnp.float32)
    diff = pos[:, None] - pos[None, :]
    decay_intra = jnp.where(diff >= 0,
                            jnp.exp(jnp.maximum(diff, 0.0)[None] * log_gamma[:, None, None]),
                            0.0)
    xi = jnp.exp((pos[:, None] + 1.0) * log_gamma[None, :])
    zeta = jnp.exp((C - 1.0 - pos)[:, None] * log_gamma[None, :])
    gamma_c = jnp.exp(C * log_gamma)
    k = k * (dk ** -0.5)
    qc = q.reshape(B, N, C, H, dk)
    kc = k.reshape(B, N, C, H, dk)
    vc = v.reshape(B, N, C, H, dv)
    scores = jnp.einsum('bnchd,bnmhd->bnhcm', qc, kc) * decay_intra.astype(q.dtype)
    intra = jnp.einsum('bnhcm,bnmhe->bnche', scores, vc)

    def step(R, xs):
        qn, kn, vn = xs
        cross = jnp.einsum('bchd,bhde->bche', qn * xi[None, :, :, None].astype(qn.dtype),
                           R.astype(qn.dtype))
        upd = jnp.einsum('bchd,bche->bhde', kn * zeta[None, :, :, None].astype(kn.dtype), vn)
        R = gamma_c[None, :, None, None] * R + upd.astype(jnp.float32)
        return R, cross

    R0 = jnp.zeros((B, H, dk, dv), jnp.float32)
    _, cross = lax.scan(step, R0, (jnp.moveaxis(qc, 1, 0), jnp.moveaxis(kc, 1, 0),
                                   jnp.moveaxis(vc, 1, 0)))
    y = (intra + jnp.moveaxis(cross, 0, 1)).reshape(B, S, H, dv).astype(jnp.float32)
    mu = y.mean(-1, keepdims=True)
    var = jnp.square(y - mu).mean(-1, keepdims=True)
    yn = ((y - mu) * lax.rsqrt(var + GN_EPS)).reshape(B, S, H * dv).astype(g.dtype)
    return yn * jax.nn.silu(g)

def dsa_attention(q, k, v, qi, ki, wi):
    B, S, H, hd = q.shape
    K = min(TOPK_MAX, S // 4)
    NB = S // Q_BLOCK
    key_pos = jnp.arange(S)
    idx_scale = (IDX_DIM ** -0.5) * (N_IDX_HEADS ** -0.5)
    gather = jax.vmap(lambda a, i: a[i])

    def block(xs):
        qb, qib, wib, t0 = xs
        t = t0 + jnp.arange(Q_BLOCK)
        rel = jax.nn.relu(jnp.einsum('bthd,bsd->bths', qib, ki).astype(jnp.float32))
        score = jnp.einsum('bths,bth->bts', rel, wib.astype(jnp.float32)) * idx_scale
        visible = key_pos[None, None, :] <= t[None, :, None]
        score = jnp.where(visible, score, -jnp.inf)
        _, sel = lax.top_k(score, K)
        k_sel = gather(k, sel)
        v_sel = gather(v, sel)
        s = jnp.einsum('bthd,btkd->bthk', qb, k_sel).astype(jnp.float32) * (hd ** -0.5)
        valid = (sel <= t[None, :, None])[:, :, None, :]
        p = jax.nn.softmax(jnp.where(valid, s, -jnp.inf), axis=-1)
        return jnp.einsum('bthk,btkd->bthd', p.astype(v.dtype), v_sel)

    def to_blocks(a):
        return jnp.moveaxis(a.reshape((B, NB, Q_BLOCK) + a.shape[2:]), 1, 0)

    out = lax.map(block, (to_blocks(q), to_blocks(qi), to_blocks(wi),
                          jnp.arange(NB) * Q_BLOCK))
    return jnp.moveaxis(out, 0, 1).reshape(B, S, H * hd)

def hybrid_mixer(x, w_in, w_ret_o, w_dsa_o, w_out):
    B, S, _ = x.shape
    pos = jnp.arange(S)
    proj = x @ w_in
    offsets = [int(o) for o in np.cumsum(COL_SIZES)[:-1]]
    rq, rk, rv, rg, aq, ak, av, iq, ik, iw, gr, ga = jnp.split(proj, offsets, axis=-1)
    rq = rotary(rq.reshape(B, S, N_RET_HEADS, RET_QK_DIM), pos)
    rk = rotary(rk.reshape(B, S, N_RET_HEADS, RET_QK_DIM), pos)
    rv = rv.reshape(B, S, N_RET_HEADS, RET_V_DIM)
    aq = rotary(aq.reshape(B, S, N_ATT_HEADS, ATT_HEAD_DIM), pos)
    ak = rotary(ak[:, :, None, :], pos)[:, :, 0]
    iq = rotary(iq.reshape(B, S, N_IDX_HEADS, IDX_DIM), pos)
    ik = rotary(ik[:, :, None, :], pos)[:, :, 0]
    ret = retention(rq, rk, rv, rg)
    att = dsa_attention(aq, ak, av, iq, ik, iw)
    merged = jax.nn.sigmoid(gr) * (ret @ w_ret_o) + jax.nn.sigmoid(ga) * (att @ w_dsa_o)
    return merged @ w_out

def hierarchical_moe(h, grp_w, grp_b, exp_w, exp_b, w_gate, w_up, w_down):
    B, S, D = h.shape
    T = B * S
    xt = h.reshape(T, D)
    grp_logits = (xt @ grp_w + grp_b).astype(jnp.float32)
    grp_prob = jax.nn.softmax(grp_logits, axis=-1)
    _, g_sel = lax.top_k(grp_logits, 1)
    p_grp = jnp.take_along_axis(grp_prob, g_sel, axis=1)
    exp_logits = (xt @ exp_w + exp_b).astype(jnp.float32).reshape(T, N_GROUPS, EXPERTS_PER_GROUP)
    in_grp = jnp.take_along_axis(exp_logits, g_sel[:, :, None], axis=1)[:, 0]
    top_logit, top_idx = lax.top_k(in_grp, TOP_K_EXPERTS)
    gate = p_grp * jax.nn.softmax(top_logit, axis=-1)
    expert = g_sel * EXPERTS_PER_GROUP + top_idx
    A = T * TOP_K_EXPERTS
    e_flat = expert.reshape(A)
    tok = jnp.repeat(jnp.arange(T), TOP_K_EXPERTS)
    w_flat = gate.reshape(A)
    order = jnp.argsort(e_flat)
    e_s, tok_s, w_s = e_flat[order], tok[order], w_flat[order]
    counts = jnp.zeros((N_EXPERTS,), jnp.int32).at[e_flat].add(1)
    starts = jnp.cumsum(counts) - counts
    padded = (counts + DISPATCH_BLOCK - 1) // DISPATCH_BLOCK * DISPATCH_BLOCK
    pad_ends = jnp.cumsum(padded)
    pad_starts = pad_ends - padded
    dest = pad_starts[e_s] + jnp.arange(A) - starts[e_s]
    n_blocks = -(-A // DISPATCH_BLOCK) + N_EXPERTS
    x_pad = jnp.zeros((n_blocks * DISPATCH_BLOCK, D), h.dtype).at[dest].set(xt[tok_s])
    block_expert = jnp.minimum(
        jnp.searchsorted(pad_ends, jnp.arange(n_blocks) * DISPATCH_BLOCK, side='right'),
        N_EXPERTS - 1)

    def expert_block(args):
        xb, e = args
        return (jax.nn.silu(xb @ w_gate[e]) * (xb @ w_up[e])) @ w_down[e]

    y_pad = lax.map(expert_block, (x_pad.reshape(n_blocks, DISPATCH_BLOCK, D), block_expert))
    y = y_pad.reshape(-1, D)[dest] * w_s[:, None].astype(h.dtype)
    return jax.ops.segment_sum(y, tok_s, num_segments=T).reshape(B, S, D)

def setup_inputs(seed: int = 0) -> dict:
    key = jax.random.key(seed)
    ks = jax.random.split(key, 17)

    def normal(k, shape, scale):
        return jax.random.normal(k, shape, jnp.float32) * scale

    ef = (DEPTH, N_EXPERTS, D_MODEL, EXPERT_FF)
    return {
        'x': normal(ks[0], (BATCH, SEQ, D_MODEL), 1.0),
        'w_in': normal(ks[1], (DEPTH, D_MODEL, IN_WIDTH), D_MODEL ** -0.5),
        'w_ret_o': normal(ks[2], (DEPTH, RET_V_W, D_MODEL), RET_V_W ** -0.5),
        'w_dsa_o': normal(ks[3], (DEPTH, ATT_Q_W, D_MODEL), ATT_Q_W ** -0.5),
        'w_out': normal(ks[4], (DEPTH, D_MODEL, D_MODEL), D_MODEL ** -0.5 * DEEPNORM_BETA),
        'ln1_g': 1.0 + normal(ks[5], (DEPTH, D_MODEL), 0.02),
        'ln1_b': normal(ks[6], (DEPTH, D_MODEL), 0.02),
        'router_grp_w': normal(ks[7], (DEPTH, D_MODEL, N_GROUPS), D_MODEL ** -0.5),
        'router_grp_b': normal(ks[8], (DEPTH, N_GROUPS), 0.01),
        'router_exp_w': normal(ks[9], (DEPTH, D_MODEL, N_EXPERTS), D_MODEL ** -0.5),
        'router_exp_b': normal(ks[10], (DEPTH, N_EXPERTS), 0.01),
        'w_gate': normal(ks[11], ef, D_MODEL ** -0.5),
        'w_up': normal(ks[12], ef, D_MODEL ** -0.5),
        'w_down': normal(ks[13], (DEPTH, N_EXPERTS, EXPERT_FF, D_MODEL),
                         EXPERT_FF ** -0.5 * DEEPNORM_BETA),
        'ln2_g': 1.0 + normal(ks[14], (DEPTH, D_MODEL), 0.02),
        'ln2_b': normal(ks[15], (DEPTH, D_MODEL), 0.02),
    }

def reference(x, w_in, w_ret_o, w_dsa_o, w_out, ln1_g, ln1_b, router_grp_w, router_grp_b,
              router_exp_w, router_exp_b, w_gate, w_up, w_down, ln2_g, ln2_b):
    for l in range(DEPTH):
        mix = hybrid_mixer(x, w_in[l], w_ret_o[l], w_dsa_o[l], w_out[l])
        h = layer_norm(DEEPNORM_ALPHA * x + mix, ln1_g[l], ln1_b[l])
        ffn = hierarchical_moe(h, router_grp_w[l], router_grp_b[l], router_exp_w[l],
                               router_exp_b[l], w_gate[l], w_up[l], w_down[l])
        x = layer_norm(DEEPNORM_ALPHA * h + ffn, ln2_g[l], ln2_b[l])
    return x


_drawn_inputs = setup_inputs


def setup_inputs(seed=0):
    import zlib

    import numpy as np

    out = dict(_drawn_inputs(seed))
    spreads = {}
    factors = {'router_grp_b': 7.997, 'router_exp_b': 14.804}
    for name, (base, spread) in spreads.items():
        noise = np.random.default_rng([zlib.crc32(name.encode()), seed]).standard_normal(out[name].shape)
        drawn = base * np.exp(spread * noise) if base else spread * noise
        out[name] = __import__('jax').numpy.asarray(drawn.astype(out[name].dtype))
    for name, factor in factors.items():
        out[name] = (out[name] * factor).astype(out[name].dtype)
    return out
```

```python
import numpy as np
import concourse.bass as bass
from concourse import mybir
from contextlib import ExitStack

P = 128
SEQ, D = 256, 1024
TT = SEQ // P
DEPTH = 2
RH, RQK, RV = 4, 256, 512
AH, AD = 8, 128
IH, ID = 8, 64
TOPK = min(256, SEQ // 4)
NG, EPG = 4, 8
NE = NG * EPG
FF = 512
KC = D // P
FC = FF // P
NB = 512
EPS = 1e-5
ALPHA = (2 * DEPTH) ** 0.25
IDX_SCALE = (ID ** -0.5) * (IH ** -0.5)
BIG = 1e30
TAKEN = -3e38
SLOTS = 64
PAIRS = NE // 2
RING = 6
TILE = KC * NB

SIZES = dict(rq=RH * RQK, rk=RH * RQK, rv=RH * RV, rg=RH * RV, aq=AH * AD, ak=AD, av=AD,
             iq=IH * ID, ik=ID, iw=IH, gr=D, ga=D)
COL = dict(zip(SIZES, np.cumsum([0, *SIZES.values()]).tolist()))

IN_TILES = [("ikw", COL["ik"], ID + IH), ("iq", COL["iq"], NB), ("ak", COL["ak"], 2 * AD)]
IN_TILES += [(f"{n}{i}", COL[n] + i * NB, NB) for n in ("aq", "rq", "rk", "rv", "rg", "gr", "ga")
             for i in range(SIZES[n] // NB)]
IN_TILE = {n: (c, w) for n, c, w in IN_TILES}
TILES = [n for n, _, _ in IN_TILES] + ["dsa0", "dsa1", "ret00", "ret01", "ret10", "ret11",
                                       "out0", "out1", "router"]
assert len(TILES) % RING == 0 and (6 * PAIRS) % RING == 0

JOBS = """XT0a XT1a Pikwv Piqv Tikwa Pakv Tiqa Paq0v Taka IX0v IX1v Paq1v Taq0a IX2v IX3v
Prq0v Taq1a Prq1v Trq0a Prk0v Trq1a Prk1v Trk0a Prv0a Trk1a AS0v Prv1a AT0a AS1v Prv2a AO0a AT1a
AS2v Prv3a AO1a AT2a AS3v Prg0a AO2a AT3a RS0v RS1v Prg1a AO3a Prg2a RY0v Prg3a RY1v Pgr0a RT0a
RY2v Pgr1a RT1a RY3v Pga0a RT2a Pga1a RT3a DO0v DO1v RO0v RO1v MT0a MT1a OUT0v OUT1v HT0a HT1a
RLv PCv""".split()
JOB = {j[:-1]: n for n, j in enumerate(JOBS)}
READER = {j[:-1]: j[-1] for j in JOBS}
GROUPS = 4

TABLES = dict(cos=TT * P, sin=TT * P, ident=P, before=P, ones=P, decay=RH * SEQ, causal=P + SEQ,
              iota=SLOTS, passes=4)
TAB = dict(zip(TABLES, np.cumsum([0, *TABLES.values()]).tolist()))
TAB_W = sum(TABLES.values())


def constant_table():
    f = np.float32
    t = np.zeros((P, TAB_W), f)

    def put(name, a):
        t[:, TAB[name]:TAB[name] + TABLES[name]] = a

    inv = (f(1) / (f(10000.0) ** (np.arange(0, RQK, 2, dtype=f) / f(RQK)))).astype(f)
    ang = np.arange(SEQ, dtype=f)[:, None] * inv[None, :]
    for name, fn in (("cos", np.cos), ("sin", np.sin)):
        put(name, fn(ang).astype(f).reshape(TT, P, P).transpose(1, 0, 2).reshape(P, -1))
    i = np.arange(P)
    put("ident", np.eye(P))
    put("before", i[:, None] < i[None, :])
    put("ones", 1)
    gamma = 1.0 - 2.0 ** (-5.0 - np.arange(RH))
    diff = np.arange(SEQ)[None, :] - i[:, None]
    decay = np.where(diff >= 0, gamma[:, None, None] ** np.maximum(diff, 0), 0) * RQK ** -0.5
    put("decay", decay.transpose(1, 0, 2).reshape(P, -1))
    hidden = np.concatenate([i[None, :] > i[:, None],
                             np.arange(SEQ)[None, :] > i[:, None] + P], axis=1)
    put("causal", np.where(hidden, -BIG, 0))
    put("iota", np.arange(SLOTS))
    put("passes", np.arange(4) * SLOTS)
    return t


def build(nc, x_in, w_in, w_ret_o, w_dsa_o, w_out, ln1_g, ln1_b, grp_w, grp_b, exp_w, exp_b,
          w_gate, w_up, w_down, ln2_g, ln2_b, tables, out):
    f32, bf16, i32, u32 = mybir.dt.float32, mybir.dt.bfloat16, mybir.dt.int32, mybir.dt.uint32
    ALU, ACT, X = mybir.AluOpType, mybir.ActivationFunctionType, mybir.AxisListType.X

    ctx = ExitStack()
    with ctx:
        def sb(name, shape, dt=f32):
            return ctx.enter_context(nc.sbuf_tensor(name, shape, dt))

        def sem(name):
            return ctx.enter_context(nc.semaphore(name))

        ring = sb("ring", [P, RING, TILE])
        tab = sb("tab", [P, TAB_W])
        x = sb("x", [P, TT, D])
        xT = sb("xT", [P, KC, SEQ])
        h = sb("h", [P, TT, D])
        qk = sb("qk", [P, RH, 4, SEQ])
        rv = sb("rv", [P, TT, RH * RV])
        rg = sb("rg", [P, RH, TT, RV])
        aqT = sb("aqT", [P, AH, SEQ])
        stage = sb("stage", [P, 2, TT, NB])
        tmp = sb("tmp", [P, TT, NB])
        sig = sb("sig", [P, TT, NB])
        akT = sb("akT", [P, SEQ])
        av = sb("av", [P, TT, AD])
        mask = sb("mask", [P, P + SEQ])
        wsc = sb("wsc", [P, TT, IH])
        rb = sb("rb", [P, NG + NE])
        m8 = sb("m8", [P, 8])
        i8 = sb("i8", [P, 8], u32)
        stat = sb("stat", [P, TT, 2, 6])
        mv = sb("mv", [P, TT, 2])
        var = sb("var", [P, TT])
        rstd = sb("rstd", [P, TT])
        nwt = sb("nwt", [P, TT])
        nmx = sb("nmx", [P, 4])
        ssum = sb("ssum", [P, 4])
        lg = sb("lg", [P, TT, NG + NE])
        g8 = sb("g8", [P, TT, 8])
        ml = sb("ml", [P, TT, NE])
        e4 = sb("e4", [P, TT, NG])
        gs = sb("gs", [P, TT, 12])
        oh = sb("oh", [P, TT, 2, NE])
        sel = sb("sel", [P, TT, NE])
        gate = sb("gate", [P, TT, NE])
        pos = sb("pos", [P, TT, NE])
        cnt = sb("cnt", [P, 6])
        npass = sb("npass", [P, 1], i32)

        def table(name, lo=0, hi=None):
            return tab[:, TAB[name] + lo:TAB[name] + (TABLES[name] if hi is None else hi)]

        ident = table("ident")
        iota = table("iota")
        causal = table("causal")

        rg_flat = rg[:, :, :, :].rearrange("p a t n -> p (a t n)")
        iqT = rg_flat[:, 0:1024].rearrange("p (b s) -> p b s", s=SEQ)
        ikT = rg_flat[:, 1024:1280]
        score = rg_flat[:, 1280:1280 + P + SEQ]
        prob = rg_flat[:, 1792:3328].rearrange("p (b a s) -> p b a s", b=2, a=2)
        pT = rg_flat[:, 3328:4096].rearrange("p (a s) -> p a s", a=2)
        stage_flat = stage[:, :, :, :].rearrange("p b t n -> p (b t n)")
        dT = stage_flat[:, 0:RH * (P + SEQ)].rearrange("p (a s) -> p a s", a=RH)
        lnp = stage_flat.rearrange("p (c n) -> p c n", c=2)
        retT = qk[:, :, :, :].rearrange("p a c s -> p (a c) s")
        mergedT = aqT
        ga = rv[:, :, 0:D]
        qk_flat = qk[:, :, :, :].rearrange("p a c s -> p (a c s)")
        xgT = qk_flat[:, 0:1024].rearrange("p (e k s) -> p e k s", e=2, k=KC)
        hT = qk_flat[:, 1024:1536].rearrange("p (e j s) -> p e j s", e=2, j=FC)
        yT = qk_flat[:, 1536:2560].rearrange("p (k s) -> p k s", k=KC)
        ytok = qk_flat[:, 2560:3584]
        gT = qk_flat[:, 3584:3840]
        aq_flat = aqT[:, :, :].rearrange("p a s -> p (a s)")
        pick = aq_flat[:, 0:256].rearrange("p (e t s) -> p e t s", e=2, t=TT)
        gpick = aq_flat[:, 256:512].rearrange("p (t s) -> p t s", t=TT)
        msig = aq_flat[:, 512:1024].rearrange("p (e s) -> p e s", e=2)
        zeros = aq_flat[:, 1280:1280 + NB // 2].bitcast(bf16)

        psum = ctx.enter_context(nc.psum_tensor("psum", [P, 8, NB], f32))

        def banks(name):
            g = JOB[name] % GROUPS
            return psum[:, 2 * g:2 * g + 2, :]

        acc = psum[:, 0:4, :].rearrange("p (t n) c -> p t (n c)", t=TT)
        A, B, C, E = (psum[:, b, :] for b in (4, 5, 6, 7))

        job_free = [sem(f"job_free{g}") for g in range(GROUPS)]
        full_a = [sem(f"full_a{g}") for g in range(GROUPS)]
        full_v = [sem(f"full_v{g}") for g in range(GROUPS)]
        tile_in = [sem(f"tile_in{s}") for s in range(RING)]
        tile_used = sem("tile_used")
        start_in = sem("start_in")
        x_ready = sem("x_ready")
        staged = sem("staged")
        dve_step = sem("dve_step")
        act_step = sem("act_step")
        max_ready = sem("max_ready")
        exp_ready = sem("exp_ready")
        p_ready = sem("p_ready")
        sig_ready = sem("sig_ready")
        sig_free = sem("sig_free")
        decayed = sem("decayed")
        yn_ready = sem("yn_ready")
        gates_in = sem("gates_in")
        merged_ready = sem("merged_ready")
        lnp_in = sem("lnp_in")
        rb_in = sem("rb_in")
        h_ready = sem("h_ready")
        router_max = sem("router_max")
        router_exp = sem("router_exp")
        sel_ready = sem("sel_ready")
        npass_pe, npass_act, npass_sp = sem("npass_pe"), sem("npass_act"), sem("npass_sp")
        picked, gpicked = sem("picked"), sem("gpicked")
        xg_full = [sem(f"xg_full{e}") for e in range(2)]
        xg_copied = [sem(f"xg_copied{e}") for e in range(2)]
        gu_full = [sem(f"gu_full{e}") for e in range(2)]
        msig_ready = [sem(f"msig_ready{e}") for e in range(2)]
        act_done = [sem(f"act_done{e}") for e in range(2)]
        yt_full = [sem(f"yt_full{e}") for e in range(2)]
        yt_copied = [sem(f"yt_copied{e}") for e in range(2)]
        ty_full = [sem(f"ty_full{n}") for n in range(2)]
        ty_copied = [sem(f"ty_copied{n}") for n in range(2)]
        tg_full, tg_copied = sem("tg_full"), sem("tg_copied")
        acc_full = sem("acc_full")
        out_in = sem("out_in")

        block = ctx.enter_context(nc.Block())

        win_v = w_in.rearrange("l (p k) n -> l p k n", k=KC)
        ret_v = w_ret_o.rearrange("l (k p) n -> l p k n", p=P)
        dsa_v = w_dsa_o.rearrange("l (k p) n -> l p k n", p=P)
        out_v = w_out.rearrange("l (k p) n -> l p k n", p=P)
        grp_v = grp_w.rearrange("l (p k) n -> l p k n", k=KC)
        exp_v = exp_w.rearrange("l (p k) n -> l p k n", k=KC)
        gate_v = w_gate.rearrange("l e (p k) n -> (l e) p (k n)", k=KC)
        up_v = w_up.rearrange("l e (p k) n -> (l e) p (k n)", k=KC)
        down_v = w_down.rearrange("l e (j p) n -> (l e) p j n", p=P)

        def slot(i, w=NB):
            return ring[:, i % RING, 0:KC * w].rearrange("p (k n) -> p k n", k=KC)

        @block.sync
        def _(sp):
            def at(v, l):
                return v[bass.ds(l, 1)].rearrange("a p k n -> p (a k) n")

            def pair(e):
                for n in range(2):
                    for u, v in enumerate((gate_v, up_v)):
                        sp.wait_ge(tile_used, 1).then_inc(tile_used, -1)
                        sp.dma_start(ring[:, 2 * n + u, :],
                                     v[bass.ds(e + n, 1)].rearrange("a p n -> p (a n)")
                                     ).then_inc(tile_in[2 * n + u], 16)
                for n in range(2):
                    sp.wait_ge(tile_used, 1).then_inc(tile_used, -1)
                    sp.dma_start(ring[:, 4 + n, :].rearrange("p (j n) -> p j n", j=FC),
                                 down_v[bass.ds(e + n, 1)].rearrange("a p j n -> p (a j) n")
                                 ).then_inc(tile_in[4 + n], 16)

            with sp.Fori(0, DEPTH) as l:
                for i, name in enumerate(TILES):
                    sp.wait_ge(tile_used, 1).then_inc(tile_used, -1)
                    landed = tile_in[i % RING]
                    if name in IN_TILE:
                        c, w = IN_TILE[name]
                        sp.dma_start(slot(i, w), at(win_v, l)[:, :, c:c + w]).then_inc(landed, 16)
                    elif name == "router":
                        sp.dma_start(slot(i, NG + NE)[:, :, 0:NG], at(grp_v, l)).then_inc(landed, 16)
                        sp.dma_start(slot(i, NG + NE)[:, :, NG:], at(exp_v, l)).then_inc(landed, 16)
                    else:
                        v = {"dsa": dsa_v, "ret": ret_v, "out": out_v}[name[:3]]
                        n = int(name[3])
                        k = KC * int(name[4]) if name[:3] == "ret" else 0
                        sp.dma_start(slot(i), at(v, l)[:, k:k + KC, n * NB:(n + 1) * NB]
                                     ).then_inc(landed, 16)
                pair(l * NE)
                sp.wait_ge(npass_sp, 1).then_inc(npass_sp, -1)
                passes = sp.value_load(npass[0:1, 0:1], min_val=1, max_val=SEQ // SLOTS)
                with sp.Fori(1, passes * PAIRS) as q:
                    pair(l * NE + (q % PAIRS) * 2)
            sp.wait_ge(x_ready, 1).then_inc(x_ready, -1)
            sp.dma_start(out.rearrange("o (t p) n -> p (o t) n", p=P), x[:, :, :]
                         ).then_inc(out_in, 16)
            sp.wait_ge(out_in, 16)

        @block.tensor
        def _(pe):
            def begin(name):
                g = JOB[name] % GROUPS
                pe.wait_ge(job_free[g], 1).then_inc(job_free[g], -1)
                return psum[:, 2 * g:2 * g + 2, :]

            def finish(name, ins):
                full = full_a if READER[name] == "a" else full_v
                ins.then_inc(full[JOB[name] % GROUPS], 1)

            def copied(name, before):
                if JOB[before] - JOB[name] <= GROUPS:
                    pe.wait_ge(job_free[JOB[name] % GROUPS], 1)

            def product(name, lhs, tiles, w=NB):
                ps = begin(name)
                for n, (tile, lt) in enumerate(zip(tiles, lhs)):
                    i = TILES.index(tile)
                    need = 32 if tile == "router" else 16
                    pe.wait_ge(tile_in[i % RING], need).then_inc(tile_in[i % RING], -need)
                    for t in range(TT):
                        for k in range(KC):
                            mm = nc.tensor.matmul(ps[:, t, 0:w], lt[:, k, t * P:(t + 1) * P],
                                                  slot(i, w)[:, k, :],
                                                  start=(n == 0 and k == 0),
                                                  stop=(n == len(tiles) - 1 and k == KC - 1),
                                                  skip_group_check=len(tiles) > 1)
                            if t == 0 and k == 0:
                                mm.then_inc(tile_used, 1)
                finish(name, mm)

            def project(tile):
                product("P" + tile, [xT], [tile], IN_TILE[tile][1])

            def transposes(name, src, n=4):
                ps = begin(name)
                v = ps.rearrange("p b c -> p (b c)")
                for j in range(n):
                    for t in range(TT):
                        o = v[:, j * SEQ + t * P:j * SEQ + (t + 1) * P]
                        mm = nc.tensor.transpose(o, src(t, j), ident)
                finish(name, mm)

            def turn_stage(tile, b, n=4):
                pe.wait_ge(staged, 1).then_inc(staged, -1)
                transposes("T" + tile, lambda t, j: stage[:, b, t, j * P:(j + 1) * P], n)

            def index_scores(i):
                if i == 0:
                    copied("Tiq", "IX0")
                ps = begin(f"IX{i}")
                for a in range(2):
                    r = slice(a * ID, (a + 1) * ID)
                    for t in range(TT):
                        mm = nc.tensor.matmul(ps[:, a, t * P:P + t * SEQ], iqT[r, i, t * P:(t + 1) * P],
                                              ikT[r, 0:(t + 1) * P], start=True, stop=True)
                finish(f"IX{i}", mm)

            def attention_scores(i):
                ps = begin(f"AS{i}")
                for a in range(2):
                    for t in range(TT):
                        mm = nc.tensor.matmul(ps[:, a, t * P:t * P + (t + 1) * P],
                                              aqT[:, 2 * i + a, t * P:(t + 1) * P],
                                              akT[:, 0:(t + 1) * P], start=True, stop=True)
                finish(f"AS{i}", mm)

            def turn_probs(i):
                pe.wait_ge(p_ready, 1).then_inc(p_ready, -1)
                ps = begin(f"AT{i}")
                for a in range(2):
                    for b in range(3):
                        mm = nc.tensor.transpose(ps[:, a, b * P:(b + 1) * P],
                                                 prob[:, i % 2, a, b * P:(b + 1) * P], ident)
                finish(f"AT{i}", mm)

            def attend(i):
                copied(f"AT{i}", f"AO{i}")
                ps = begin(f"AO{i}").rearrange("p b c -> p (b c)")
                for a in range(2):
                    o = ps[:, a * SEQ:(a + 1) * SEQ]
                    nc.tensor.matmul(o[:, 0:P], av[:, 0, :], pT[:, a, 0:P], start=True, stop=True)
                    nc.tensor.matmul(o[:, P:SEQ], av[:, 0, :], pT[:, a, P:SEQ],
                                     start=True, stop=False)
                    mm = nc.tensor.matmul(o[:, P:SEQ], av[:, 1, :], pT[:, a, SEQ:SEQ + P],
                                          start=False, stop=True)
                finish(f"AO{i}", mm)

            def retention_scores(i):
                ps = begin(f"RS{i}")
                for a in range(2):
                    q = qk[:, 2 * i + a, 0:2, :]
                    k = qk[:, 2 * i + a, 2:4, :]
                    for m, (lo, hi) in enumerate(((0, SEQ), (SEQ, SEQ + P))):
                        for c in range(2):
                            mm = nc.tensor.matmul(ps[:, a, lo:hi], k[:, c, m * P:(m + 1) * P],
                                                  q[:, c, m * P:SEQ], start=(c == 0), stop=(c == 1))
                finish(f"RS{i}", mm)

            def retention_values(i):
                if i % 2 == 0:
                    pe.wait_ge(decayed, 1).then_inc(decayed, -1)
                ps = begin(f"RY{i}")
                v = rv[:, :, i * RV:(i + 1) * RV]
                nc.tensor.matmul(ps[:, 0, :], dT[:, i, 0:P], v[:, 0, :], start=True, stop=True)
                nc.tensor.matmul(ps[:, 1, :], dT[:, i, P:SEQ], v[:, 0, :], start=True, stop=False)
                mm = nc.tensor.matmul(ps[:, 1, :], dT[:, i, SEQ:SEQ + P], v[:, 1, :],
                                      start=False, stop=True)
                finish(f"RY{i}", mm)

            def turn_retention(i):
                pe.wait_ge(yn_ready, 1).then_inc(yn_ready, -1)
                transposes(f"RT{i}", lambda t, j: rg[:, i, t, j * P:(j + 1) * P])

            def experts(first):
                if not first:
                    turn_gates()
                pe.wait_ge(picked, 1).then_inc(picked, -1)
                if not first:
                    for e in range(2):
                        pe.wait_ge(yt_copied[e], 1).then_inc(yt_copied[e], -1)
                for e, bank in enumerate((A, B)):
                    for k in range(KC):
                        for t in range(TT):
                            mm = nc.tensor.matmul(bank[:, k * SLOTS:(k + 1) * SLOTS],
                                                  h[:, t, k:D:KC], pick[:, e, t, :],
                                                  start=(t == 0), stop=(t == TT - 1))
                    mm.then_inc(xg_full[e], 1)
                if not first:
                    pe.wait_ge(tg_copied, 1).then_inc(tg_copied, -1)
                pe.wait_ge(xg_copied[0], 1).then_inc(xg_copied[0], -1)
                gate_up(0, C)
                pe.wait_ge(xg_copied[1], 1).then_inc(xg_copied[1], -1)
                if not first:
                    turn_y()
                gate_up(1, E)
                if not first:
                    combine()
                for e, bank in enumerate((A, B)):
                    pe.wait_ge(act_done[e], 1).then_inc(act_done[e], -1)
                    s = 4 + e
                    pe.wait_ge(tile_in[s], 16).then_inc(tile_in[s], -16)
                    wd = ring[:, s, :].rearrange("p (j n) -> p j n", j=FC)
                    for k in range(KC):
                        for j in range(FC):
                            mm = nc.tensor.matmul(bank[:, k * SLOTS:(k + 1) * SLOTS],
                                                  wd[:, j, k * P:(k + 1) * P], hT[:, e, j, :],
                                                  start=(j == 0), stop=(j == FC - 1))
                            if k == 0 and j == 0:
                                mm.then_inc(tile_used, 1)
                    mm.then_inc(yt_full[e], 1)

            def gate_up(e, bank):
                for u in range(2):
                    s = 2 * e + u
                    pe.wait_ge(tile_in[s], 16).then_inc(tile_in[s], -16)
                    w = ring[:, s, :].rearrange("p (k n) -> p k n", k=KC)
                    for j in range(FC):
                        c = (u * FC + j) * SLOTS
                        for k in range(KC):
                            mm = nc.tensor.matmul(bank[:, c:c + SLOTS], w[:, k, j * P:(j + 1) * P],
                                                  xgT[:, e, k, :], start=(k == 0),
                                                  stop=(k == KC - 1))
                            if k == 0 and j == 0:
                                mm.then_inc(tile_used, 1)
                mm.then_inc(gu_full[e], 1)

            def turn_gates():
                pe.wait_ge(gpicked, 1).then_inc(gpicked, -1)
                for t in range(TT):
                    mm = nc.tensor.transpose(C[:, t * P:(t + 1) * P], gpick[:, t, :], ident)
                mm.then_inc(tg_full, 1)

            def turn_y():
                for n, bank in enumerate((A, B)):
                    for k in range(4):
                        mm = nc.tensor.transpose(bank[:, k * P:(k + 1) * P], yT[:, 4 * n + k, :],
                                                 ident)
                    mm.then_inc(ty_full[n], 1)

            def combine():
                for n in range(2):
                    pe.wait_ge(ty_copied[n], 1).then_inc(ty_copied[n], -1)
                for t in range(TT):
                    for n in range(2):
                        nc.tensor.matmul(acc[:, t, n * NB:(n + 1) * NB], gT[:, t * P:(t + 1) * P],
                                         ytok[:, n * NB:(n + 1) * NB], start=False, stop=False,
                                         skip_group_check=True)

            with pe.Fori(0, DEPTH) as l:
                pe.wait_ge(x_ready, 1).then_inc(x_ready, -1)
                for i in range(2):
                    transposes(f"XT{i}", lambda t, j: x[:, t, 4 * i + j:D:KC])
                copied("XT0", "Pikw")
                copied("XT1", "Pikw")
                project("ikw")
                project("iq")
                turn_stage("ikw", 0, 1)
                project("ak")
                turn_stage("iq", 1)
                project("aq0")
                turn_stage("ak", 0, 1)
                index_scores(0)
                index_scores(1)
                project("aq1")
                turn_stage("aq0", 1)
                index_scores(2)
                index_scores(3)
                project("rq0")
                turn_stage("aq1", 0)
                project("rq1")
                turn_stage("rq0", 1)
                project("rk0")
                turn_stage("rq1", 0)
                project("rk1")
                turn_stage("rk0", 1)
                project("rv0")
                turn_stage("rk1", 0)
                attention_scores(0)
                project("rv1")
                turn_probs(0)
                attention_scores(1)
                project("rv2")
                attend(0)
                turn_probs(1)
                attention_scores(2)
                project("rv3")
                attend(1)
                turn_probs(2)
                attention_scores(3)
                project("rg0")
                attend(2)
                turn_probs(3)
                retention_scores(0)
                retention_scores(1)
                project("rg1")
                attend(3)
                project("rg2")
                retention_values(0)
                project("rg3")
                retention_values(1)
                project("gr0")
                turn_retention(0)
                retention_values(2)
                project("gr1")
                turn_retention(1)
                retention_values(3)
                project("ga0")
                turn_retention(2)
                project("ga1")
                turn_retention(3)
                product("DO0", [aqT], ["dsa0"])
                product("DO1", [aqT], ["dsa1"])
                copied("RT3", "RO0")
                for n in range(2):
                    product(f"RO{n}", [retT[:, 0:KC, :], retT[:, KC:, :]], [f"ret{n}0", f"ret{n}1"])
                for i in range(2):
                    pe.wait_ge(merged_ready, 1).then_inc(merged_ready, -1)
                    transposes(f"MT{i}", lambda t, j: h[:, t, (4 * i + j) * P:(4 * i + j + 1) * P])
                copied("MT0", "OUT0")
                copied("MT1", "OUT0")
                for n in range(2):
                    product(f"OUT{n}", [mergedT], [f"out{n}"])
                pe.wait_ge(h_ready, 1).then_inc(h_ready, -1)
                for i in range(2):
                    transposes(f"HT{i}", lambda t, j: h[:, t, 4 * i + j:D:KC])
                copied("HT0", "RL")
                copied("HT1", "RL")
                product("RL", [xT], ["router"], NG + NE)
                pe.wait_ge(sel_ready, 1).then_inc(sel_ready, -1)
                ps = begin("PC")
                nc.tensor.matmul(ps[:, 0, 0:NE], table("before"), sel[:, 0, :], start=True, stop=True)
                for c, m in ((1, "before"), (2, "ones")):
                    nc.tensor.matmul(ps[:, 0, c * NE:(c + 1) * NE], table("ones"), sel[:, 0, :],
                                     start=True, stop=False)
                    mm = nc.tensor.matmul(ps[:, 0, c * NE:(c + 1) * NE], table(m), sel[:, 1, :],
                                          start=False, stop=True)
                finish("PC", mm)
                for g in range(GROUPS):
                    pe.wait_ge(job_free[g], 1)
                pe.wait_ge(npass_pe, 1).then_inc(npass_pe, -1)
                for b in range(4):
                    nc.tensor.matmul(psum[:, b, :], zeros[:, 0:P], zeros, start=True,
                                     stop=False, skip_group_check=True)
                passes = pe.value_load(npass[0:1, 0:1], min_val=1, max_val=SEQ // SLOTS)
                with pe.Fori(0, passes) as _p:
                    experts(True)
                    with pe.Fori(1, PAIRS) as _j:
                        experts(False)
                    turn_gates()
                    for e in range(2):
                        pe.wait_ge(yt_copied[e], 1).then_inc(yt_copied[e], -1)
                    turn_y()
                    pe.wait_ge(tg_copied, 1).then_inc(tg_copied, -1)
                    combine()
                for b in range(4):
                    mm = nc.tensor.matmul(psum[:, b, :], zeros[:, 0:P], zeros, start=False,
                                          stop=True, skip_group_check=True)
                mm.then_inc(acc_full, 1)

        @block.scalar
        def _(act):
            def take(name):
                g = JOB[name] % GROUPS
                act.wait_ge(full_a[g], 1).then_inc(full_a[g], -1)
                return psum[:, 2 * g:2 * g + 2, :]

            def copy_out(name, dst, n=1024):
                src = take(name).rearrange("p b c -> p (b c)")[:, 0:n]
                if len(dst.shape) == 3:
                    src = src.rearrange("p (a b) -> p a b", a=dst.shape[1])
                elif len(dst.shape) == 4:
                    src = src.rearrange("p (a b c) -> p a b c", a=dst.shape[1], b=dst.shape[2])
                nc.scalar.activation(dst, src, ACT.Copy).then_inc(job_free[JOB[name] % GROUPS], 1)

            def exps(i):
                act.wait_ge(max_ready, 1).then_inc(max_ready, -1)
                for a in range(2):
                    for t in range(TT):
                        v = prob[:, i % 2, a, t * P:P + t * SEQ]
                        e = nc.scalar.activation(v, v, ACT.Exp, bias=nmx[:, 2 * t + a:2 * t + a + 1],
                                                 accum_out=ssum[:, 2 * t + a:2 * t + a + 1])
                        if (a, t) != (1, TT - 1):
                            e.then_inc(act_step, 1)
                            act.wait_ge(act_step, 1).then_inc(act_step, -1)
                e.then_inc(exp_ready, 1)

            def silu_gate(n):
                ps = take(f"Prg{n}")
                act.wait_ge(sig_free, 1).then_inc(sig_free, -1)
                nc.scalar.activation(sig[:, :, :], ps, ACT.Sigmoid).then_inc(sig_ready, 1)

            def branch_gate(name, dst):
                ps = take("P" + name)
                g = JOB["P" + name] % GROUPS
                nc.scalar.activation(dst, ps, ACT.Sigmoid).then_inc(act_step, 1)
                act.wait_ge(act_step, 1).then_inc(act_step, -1)
                act.sem_inc(job_free[g], 1)
                act.sem_inc(gates_in, 1)

            def turned_y():
                for n, bank in enumerate((A, B)):
                    act.wait_ge(ty_full[n], 1).then_inc(ty_full[n], -1)
                    nc.scalar.activation(ytok[:, n * NB:(n + 1) * NB], bank, ACT.Copy
                                         ).then_inc(ty_copied[n], 1)

            def experts(first):
                for e, bank in enumerate((C, E)):
                    act.wait_ge(gu_full[e], 1).then_inc(gu_full[e], -1)
                    nc.scalar.activation(msig[:, e, :], bank[:, 0:FC * SLOTS], ACT.Sigmoid
                                         ).then_inc(msig_ready[e], 1)
                    if e == 0 and not first:
                        turned_y()
                for e, bank in enumerate((A, B)):
                    act.wait_ge(yt_full[e], 1).then_inc(yt_full[e], -1)
                    nc.scalar.activation(yT[:, :, e * SLOTS:(e + 1) * SLOTS],
                                         bank.rearrange("p (k s) -> p k s", k=KC), ACT.Copy
                                         ).then_inc(yt_copied[e], 1)

            def ln_params(g, b, l):
                for n, v in enumerate((g, b)):
                    act.dma_start(lnp[:, n, :], v[bass.ds(l, 1)].broadcast_to((P, D))
                                  ).then_inc(lnp_in, 16)

            act.dma_start(x[:, :, :], x_in.rearrange("o (t p) n -> p (o t) n", p=P)
                          ).then_inc(start_in, 16)
            act.dma_start(tab[:, :], tables).then_inc(start_in, 16)
            with act.Fori(0, DEPTH) as l:
                act.dma_start(rb[:, 0:NG], grp_b[bass.ds(l, 1)].broadcast_to((P, NG))
                              ).then_inc(rb_in, 16)
                act.dma_start(rb[:, NG:], exp_b[bass.ds(l, 1)].broadcast_to((P, NE))
                              ).then_inc(rb_in, 16)
                copy_out("XT0", xT[:, 0:4, :])
                copy_out("XT1", xT[:, 4:8, :])
                copy_out("Tikw", ikT, SEQ)
                copy_out("Tiq", iqT)
                copy_out("Tak", akT[:, :], SEQ)
                copy_out("Taq0", aqT[:, 0:4, :])
                copy_out("Taq1", aqT[:, 4:8, :])
                copy_out("Trq0", qk[:, 0:2, 0:2, :])
                copy_out("Trq1", qk[:, 2:4, 0:2, :])
                copy_out("Trk0", qk[:, 0:2, 2:4, :])
                copy_out("Prv0", rv[:, :, 0:NB])
                copy_out("Trk1", qk[:, 2:4, 2:4, :])
                exps(0)
                for i in range(1, 4):
                    copy_out(f"Prv{i}", rv[:, :, i * NB:(i + 1) * NB])
                    if i >= 2:
                        copy_out(f"AO{i - 2}", aqT[:, 2 * i - 4:2 * i - 2, :], 2 * SEQ)
                    turned = take(f"AT{i - 1}")
                    nc.scalar.activation(pT[:, :, :], turned[:, :, 0:P + SEQ], ACT.Copy
                                         ).then_inc(job_free[JOB[f"AT{i - 1}"] % GROUPS], 1)
                    exps(i)
                silu_gate(0)
                copy_out("AO2", aqT[:, 4:6, :], 2 * SEQ)
                turned = take("AT3")
                nc.scalar.activation(pT[:, :, :], turned[:, :, 0:P + SEQ], ACT.Copy
                                     ).then_inc(job_free[JOB["AT3"] % GROUPS], 1)
                silu_gate(1)
                copy_out("AO3", aqT[:, 6:8, :], 2 * SEQ)
                silu_gate(2)
                silu_gate(3)
                branch_gate("gr0", h[:, :, 0:NB])
                copy_out("RT0", retT[:, 0:4, :])
                branch_gate("gr1", h[:, :, NB:D])
                copy_out("RT1", retT[:, 4:8, :])
                branch_gate("ga0", ga[:, :, 0:NB])
                copy_out("RT2", retT[:, 8:12, :])
                branch_gate("ga1", ga[:, :, NB:D])
                copy_out("RT3", retT[:, 12:16, :])
                ln_params(ln1_g, ln1_b, l)
                for i in range(2):
                    copy_out(f"MT{i}", mergedT[:, 4 * i:4 * i + 4, :])
                for i in range(2):
                    copy_out(f"HT{i}", xT[:, 4 * i:4 * i + 4, :])
                act.wait_ge(router_max, 1).then_inc(router_max, -1)
                ln_params(ln2_g, ln2_b, l)
                for t in range(TT):
                    nc.scalar.activation(e4[:, t, :], lg[:, t, 0:NG], ACT.Exp,
                                         bias=gs[:, t, 0:1], accum_out=gs[:, t, 1:2]
                                         ).then_inc(act_step, 1)
                    act.wait_ge(act_step, 1).then_inc(act_step, -1)
                nc.scalar.activation(gs[:, :, 3:4], gs[:, :, 2:3], ACT.Exp).then_inc(router_exp, 1)
                act.wait_ge(npass_act, 1).then_inc(npass_act, -1)
                passes = act.value_load(npass[0:1, 0:1], min_val=1, max_val=SEQ // SLOTS)
                with act.Fori(0, passes) as _p:
                    experts(True)
                    with act.Fori(1, PAIRS) as _j:
                        experts(False)
                    turned_y()

        @block.vector
        def _(dve):
            V = nc.vector

            def step(ins):
                ins.then_inc(dve_step, 1)
                dve.wait_ge(dve_step, 1).then_inc(dve_step, -1)

            def take(name):
                g = JOB[name] % GROUPS
                dve.wait_ge(full_v[g], 1).then_inc(full_v[g], -1)
                return psum[:, 2 * g:2 * g + 2, :]

            def free(name):
                dve.sem_inc(job_free[JOB[name] % GROUPS], 1)

            def rotate(name, b, half, heads):
                ps = take(name)
                w = 2 * half * heads
                for t in range(TT):
                    src = ps[:, t, 0:w].rearrange("p (a d) -> p a d", d=half)
                    for fn, dst in (("cos", tmp), ("sin", sig)):
                        f = table(fn, t * P, (t + 1) * P)[:, 0:P:P // half]
                        step(V.tensor_tensor(dst[:, t, 0:w].rearrange("p (a d) -> p a d", d=half),
                                             src, f.unsqueeze(1).broadcast_to((P, 2 * heads, half)),
                                             ALU.mult))
                for t in range(TT):
                    def halves(a):
                        v = a.rearrange("p (a c d) -> p a c d", c=2, d=half)
                        return v[:, :, 0, :], v[:, :, 1, :]
                    (c1, c2), (s1, s2) = halves(tmp[:, t, 0:w]), halves(sig[:, t, 0:w])
                    o1, o2 = halves(stage[:, b, t, 0:w])
                    V.tensor_tensor(o1, c1, s2, ALU.subtract)
                    step(V.tensor_tensor(o2, c2, s1, ALU.add))
                return ps

            def norm_stats(n):
                for t in range(TT):
                    step(V.bn_aggr(mv[:, t, :], stat[:, t, 0:n, :].rearrange("p a b -> p (a b)")))
                step(V.tensor_scalar(var[:, :], mv[:, :, 1], EPS, None, ALU.add))
                step(V.tensor_scalar(rstd[:, :].bitcast(i32), var[:, :].bitcast(i32), 1, None,
                                     ALU.logical_shift_right))
                step(V.tensor_scalar(rstd[:, :].bitcast(i32), rstd[:, :].bitcast(i32), -1.0,
                                     float(0x5F3759DF), ALU.mult, ALU.add))
                for _ in range(4):
                    step(V.tensor_tensor(nwt[:, :], rstd[:, :], rstd[:, :], ALU.mult))
                    step(V.tensor_tensor(nwt[:, :], nwt[:, :], var[:, :], ALU.mult))
                    step(V.tensor_scalar(nwt[:, :], nwt[:, :], -0.5, 1.5, ALU.mult, ALU.add))
                    step(V.tensor_tensor(rstd[:, :], rstd[:, :], nwt[:, :], ALU.mult))
                step(V.scalar_tensor_tensor(out=nwt[:, :], in0=mv[:, :, 0], scalar=-1.0,
                                            in1=rstd[:, :], op0=ALU.mult, op1=ALU.mult))

            def layer_norm(src, dst):
                for t in range(TT):
                    for n in range(2):
                        step(V.bn_stats(stat[:, t, n, :], src[:, t, n * NB:(n + 1) * NB]))
                norm_stats(2)
                dve.wait_ge(lnp_in, 32).then_inc(lnp_in, -32)
                for t in range(TT):
                    step(V.tensor_scalar(dst[:, t, :], src[:, t, :], rstd[:, t:t + 1],
                                         nwt[:, t:t + 1], ALU.mult, ALU.add))
                    step(V.tensor_tensor(dst[:, t, :], dst[:, t, :], lnp[:, 0, :], ALU.mult))
                    step(V.tensor_tensor(dst[:, t, :], dst[:, t, :], lnp[:, 1, :], ALU.add))

            def index_scores(i):
                ps = take(f"IX{i}")
                for a in range(2):
                    hd = 2 * i + a
                    for t in range(TT):
                        lo, hi = t * P, P + t * SEQ
                        step(V.tensor_scalar(tmp[:, 0, lo:hi], ps[:, a, lo:hi], 0.0,
                                             wsc[:, t, hd:hd + 1], ALU.max, ALU.mult))
                    if a == 1:
                        free(f"IX{i}")
                    prev = causal if hd == 0 else score
                    step(V.tensor_tensor(score, prev, tmp[:, 0, 0:P + SEQ], ALU.add))

            def select():
                for lo, hi in ((0, P), (P, P + SEQ)):
                    for _ in range(TOPK // 8):
                        step(V.max(m8[:, :], score[:, lo:hi]))
                        step(V.match_replace(score[:, lo:hi], m8[:, :], score[:, lo:hi], TAKEN))
                step(V.tensor_scalar(score, score, TAKEN, 1.0, ALU.is_equal, ALU.subtract))
                step(V.scalar_tensor_tensor(out=mask[:, :], in0=score, scalar=BIG, in1=causal,
                                            op0=ALU.mult, op1=ALU.min))

            def softmax(i):
                ps = take(f"AS{i}")
                pr = prob[:, i % 2, :, :]
                for a in range(2):
                    step(V.scalar_tensor_tensor(out=pr[:, a, :], in0=ps[:, a, 0:P + SEQ],
                                                scalar=AD ** -0.5, in1=mask[:, :],
                                                op0=ALU.mult, op1=ALU.add))
                free(f"AS{i}")
                for t in range(TT):
                    step(V.tensor_reduce(nmx[:, 2 * t:2 * t + 2], pr[:, :, t * P:P + t * SEQ], X,
                                         ALU.max))
                step(V.tensor_scalar(nmx[:, :], nmx[:, :], -1.0, None, ALU.mult))
                dve.sem_inc(max_ready, 1)
                dve.wait_ge(exp_ready, 1).then_inc(exp_ready, -1)
                step(V.reciprocal(ssum[:, :], ssum[:, :]))
                for a in range(2):
                    for t in range(TT):
                        v = pr[:, a, t * P:P + t * SEQ]
                        step(V.tensor_scalar(v, v, ssum[:, 2 * t + a:2 * t + a + 1], None, ALU.mult))
                dve.sem_inc(p_ready, 1)

            def silu(n):
                dve.wait_ge(sig_ready, 1).then_inc(sig_ready, -1)
                step(V.tensor_tensor(rg[:, n, :, :], banks(f"Prg{n}"), sig[:, :, :], ALU.mult))
                free(f"Prg{n}")
                dve.sem_inc(sig_free, 1)

            def decay(i):
                ps = take(f"RS{i}")
                for a in range(2):
                    hd = 2 * i + a
                    d = table("decay", hd * SEQ, (hd + 1) * SEQ)
                    step(V.tensor_tensor(dT[:, hd, 0:SEQ], ps[:, a, 0:SEQ], d, ALU.mult))
                    step(V.tensor_tensor(dT[:, hd, SEQ:SEQ + P], ps[:, a, SEQ:SEQ + P], d[:, 0:P],
                                         ALU.mult))
                free(f"RS{i}")
                dve.sem_inc(decayed, 1)

            def group_norm(i):
                ps = take(f"RY{i}")
                for t in range(TT):
                    step(V.bn_stats(stat[:, t, 0, :], ps[:, t, :]))
                norm_stats(1)
                for t in range(TT):
                    step(V.tensor_scalar(tmp[:, t, :], ps[:, t, :], rstd[:, t:t + 1],
                                         nwt[:, t:t + 1], ALU.mult, ALU.add))
                free(f"RY{i}")
                step(V.tensor_tensor(rg[:, i, :, :], rg[:, i, :, :], tmp[:, :, :], ALU.mult))
                dve.sem_inc(yn_ready, 1)

            def router():
                ps = take("RL")
                dve.wait_ge(rb_in, 32).then_inc(rb_in, -32)
                for t in range(TT):
                    step(V.tensor_tensor(lg[:, t, :], ps[:, t, 0:NG + NE], rb[:, :], ALU.add))
                free("RL")
                for t in range(TT):
                    step(V.tensor_copy(g8[:, t, 0:NG], lg[:, t, 0:NG]))
                    step(V.max(m8[:, :], g8[:, t, :]))
                    step(V.max_index(i8[:, :], m8[:, :], g8[:, t, :]))
                    step(V.tensor_scalar(gs[:, t, 0:1], m8[:, 0:1], -1.0, None, ALU.mult))
                    step(V.tensor_copy(gs[:, t, 4:5], i8[:, 0:1]))
                    step(V.tensor_scalar(oh[:, t, 0, 0:NG], iota[:, 0:NG], gs[:, t, 4:5], None,
                                         ALU.is_equal))
                    step(V.tensor_scalar(oh[:, t, 0, 0:NG], oh[:, t, 0, 0:NG], 1.0, BIG,
                                         ALU.subtract, ALU.mult))
                    step(V.tensor_tensor(
                        ml[:, t, :].rearrange("p (g e) -> p g e", g=NG),
                        lg[:, t, NG:].rearrange("p (g e) -> p g e", g=NG),
                        oh[:, t, 0, 0:NG].unsqueeze(2).broadcast_to((P, NG, EPG)), ALU.add))
                    step(V.max(m8[:, :], ml[:, t, :]))
                    step(V.max_index(i8[:, :], m8[:, :], ml[:, t, :]))
                    step(V.tensor_tensor(gs[:, t, 2:3], m8[:, 1:2], m8[:, 0:1], ALU.subtract))
                    step(V.tensor_copy(gs[:, t, 5:7], i8[:, 0:2]))
                    for c in range(2):
                        step(V.tensor_scalar(oh[:, t, c, :], iota[:, 0:NE], gs[:, t, 5 + c:6 + c],
                                             None, ALU.is_equal))
                    step(V.tensor_tensor(sel[:, t, :], oh[:, t, 0, :], oh[:, t, 1, :], ALU.add))
                dve.sem_inc(router_max, 1)
                dve.sem_inc(sel_ready, 1)
                dve.wait_ge(router_exp, 1).then_inc(router_exp, -1)
                step(V.tensor_scalar(gs[:, :, 7:8], gs[:, :, 3:4], 1.0, None, ALU.add))
                step(V.tensor_tensor(gs[:, :, 7:8], gs[:, :, 7:8], gs[:, :, 1:2], ALU.mult))
                step(V.reciprocal(gs[:, :, 7:8], gs[:, :, 7:8]))
                step(V.tensor_tensor(gs[:, :, 8:9], gs[:, :, 7:8], gs[:, :, 3:4], ALU.mult))
                for t in range(TT):
                    step(V.tensor_scalar(gate[:, t, :], oh[:, t, 0, :], gs[:, t, 7:8], None,
                                         ALU.mult))
                    step(V.scalar_tensor_tensor(out=gate[:, t, :], in0=oh[:, t, 1, :],
                                                scalar=gs[:, t, 8:9], in1=gate[:, t, :],
                                                op0=ALU.mult, op1=ALU.add))

            def places():
                ps = take("PC")
                pc = ps[:, 0, 0:3 * NE].rearrange("p (c e) -> p c e", c=3)
                for t in range(TT):
                    step(V.scalar_tensor_tensor(out=pos[:, t, :], in0=pc[:, t, :], scalar=1.0,
                                                in1=sel[:, t, :], op0=ALU.add, op1=ALU.mult))
                step(V.tensor_scalar(pos[:, :, :], pos[:, :, :], -1.0, None, ALU.add))
                step(V.tensor_reduce(cnt[:, 0:1], pc[:, 2, :], X, ALU.max))
                free("PC")
                step(V.tensor_scalar(cnt[:, 1:5], table("passes"), cnt[:, 0:1], None, ALU.is_lt))
                step(V.tensor_reduce(cnt[:, 5:6], cnt[:, 1:5], X, ALU.add))
                step(V.tensor_copy(npass[:, :], cnt[:, 5:6]))
                step(V.memset(zeros, 0.0))
                dve.sem_inc(npass_sp, 1)
                dve.sem_inc(npass_pe, 1)
                dve.sem_inc(npass_act, 1)

            def turned_gates():
                dve.wait_ge(tg_full, 1).then_inc(tg_full, -1)
                V.tensor_copy(gT, C[:, 0:SEQ]).then_inc(tg_copied, 1)

            def experts(e0, first):
                for e in range(2):
                    for t in range(TT):
                        step(V.tensor_scalar(pick[:, e, t, :], iota, pos[:, t, bass.ds(e0 + e, 1)],
                                             None, ALU.is_equal))
                dve.sem_inc(picked, 1)
                if not first:
                    turned_gates()
                for e in range(2):
                    for t in range(TT):
                        step(V.tensor_scalar(gpick[:, t, e * SLOTS:(e + 1) * SLOTS],
                                             pick[:, e, t, :], gate[:, t, bass.ds(e0 + e, 1)],
                                             None, ALU.mult))
                dve.sem_inc(gpicked, 1)
                for e, bank in enumerate((A, B)):
                    dve.wait_ge(xg_full[e], 1).then_inc(xg_full[e], -1)
                    V.tensor_copy(xgT[:, e, :, :], bank.rearrange("p (k s) -> p k s", k=KC)
                                  ).then_inc(xg_copied[e], 1)
                for e, bank in enumerate((C, E)):
                    dve.wait_ge(msig_ready[e], 1).then_inc(msig_ready[e], -1)
                    step(V.tensor_tensor(msig[:, e, :], bank[:, 0:FC * SLOTS], msig[:, e, :],
                                         ALU.mult))
                    V.tensor_tensor(hT[:, e, :, :].rearrange("p j s -> p (j s)"), msig[:, e, :],
                                    bank[:, FC * SLOTS:2 * FC * SLOTS], ALU.mult
                                    ).then_inc(act_done[e], 1)

            step(V.memset(g8[:, :, :], -BIG))
            for g in range(GROUPS):
                dve.sem_inc(job_free[g], 1)
            dve.sem_inc(tile_used, RING - 1)
            dve.sem_inc(sig_free, 1)
            dve.wait_ge(start_in, 32)
            dve.sem_inc(x_ready, 1)
            with dve.Fori(0, DEPTH) as l:
                ps = rotate("Pikw", 0, ID // 2, 1)
                for t in range(TT):
                    step(V.tensor_copy(stage[:, 0, t, ID:2 * ID], stage[:, 0, t, 0:ID]))
                step(V.tensor_scalar(wsc[:, :, :], ps[:, :, ID:ID + IH], IDX_SCALE, None, ALU.mult))
                free("Pikw")
                dve.sem_inc(staged, 1)
                rotate("Piq", 1, ID // 2, IH)
                free("Piq")
                dve.sem_inc(staged, 1)
                ps = rotate("Pak", 0, AD // 2, 1)
                step(V.tensor_copy(av[:, :, :], ps[:, :, AD:2 * AD]))
                free("Pak")
                dve.sem_inc(staged, 1)
                rotate("Paq0", 1, AD // 2, 4)
                free("Paq0")
                dve.sem_inc(staged, 1)
                index_scores(0)
                index_scores(1)
                rotate("Paq1", 0, AD // 2, 4)
                free("Paq1")
                dve.sem_inc(staged, 1)
                index_scores(2)
                index_scores(3)
                for n, name in enumerate(("rq0", "rq1", "rk0", "rk1")):
                    rotate("P" + name, (n + 1) % 2, RQK // 2, 2)
                    free("P" + name)
                    dve.sem_inc(staged, 1)
                    if n == 2:
                        select()
                for i in range(4):
                    softmax(i)
                silu(0)
                decay(0)
                decay(1)
                silu(1)
                silu(2)
                group_norm(0)
                silu(3)
                for i in range(1, RH):
                    group_norm(i)
                dve.wait_ge(gates_in, 4).then_inc(gates_in, -4)
                for n in range(2):
                    ps = take(f"DO{n}")
                    c = slice(n * NB, (n + 1) * NB)
                    step(V.tensor_tensor(ga[:, :, c], ga[:, :, c], ps, ALU.mult))
                    free(f"DO{n}")
                for n in range(2):
                    ps = take(f"RO{n}")
                    c = slice(n * NB, (n + 1) * NB)
                    step(V.tensor_tensor(h[:, :, c], h[:, :, c], ps, ALU.mult))
                    free(f"RO{n}")
                    step(V.tensor_tensor(h[:, :, c], h[:, :, c], ga[:, :, c], ALU.add))
                    dve.sem_inc(merged_ready, 1)
                for n in range(2):
                    ps = take(f"OUT{n}")
                    c = slice(n * NB, (n + 1) * NB)
                    step(V.scalar_tensor_tensor(out=x[:, :, c], in0=x[:, :, c], scalar=ALPHA,
                                                in1=ps, op0=ALU.mult, op1=ALU.add))
                    free(f"OUT{n}")
                layer_norm(x, h)
                dve.sem_inc(h_ready, 1)
                router()
                places()
                passes = dve.value_load(npass[0:1, 0:1], min_val=1, max_val=SEQ // SLOTS)
                with dve.Fori(0, passes) as _p:
                    experts(0, True)
                    with dve.Fori(1, PAIRS) as j:
                        experts(j * 2, False)
                    turned_gates()
                    step(V.tensor_scalar(pos[:, :, :], pos[:, :, :], -float(SLOTS), None, ALU.add))
                dve.wait_ge(acc_full, 1).then_inc(acc_full, -1)
                for t in range(TT):
                    step(V.scalar_tensor_tensor(out=x[:, t, :], in0=h[:, t, :], scalar=ALPHA,
                                                in1=acc[:, t, :], op0=ALU.mult, op1=ALU.add))
                layer_norm(x, x)
                dve.sem_inc(x_ready, 1)


_INS = ['x', 'w_in', 'w_ret_o', 'w_dsa_o', 'w_out', 'ln1_g', 'ln1_b', 'router_grp_w',
        'router_grp_b', 'router_exp_w', 'router_exp_b', 'w_gate', 'w_up', 'w_down', 'ln2_g',
        'ln2_b']


def kernel(**inputs):
    import concourse.bacc as _bacc
    from concourse.bass_utils import run_bass_kernel_spmd as _run

    nc = _bacc.Bacc("TRN2", target_bir_lowering=False, num_devices=1)
    arrays, args = {}, []
    given = {n: np.ascontiguousarray(inputs[n]) for n in _INS}
    for name, a in [*given.items(), ("tables", constant_table())]:
        arrays[f"in_{name}_dram"] = a
        args.append(nc.dram_tensor(f"in_{name}_dram", a.shape, mybir.dt.from_np(a.dtype),
                                   kind="ExternalInput").ap())
    args.append(nc.dram_tensor("out_0_dram", (1, SEQ, D), mybir.dt.float32,
                               kind="ExternalOutput").ap())
    build(nc, *args)
    r = _run(nc, [arrays], core_ids=[0])
    return r.results[0]["out_0_dram"]
```

```python
import numpy as np
import concourse.bass as bass
from concourse import mybir
from contextlib import ExitStack

P = 128
SEQ, D = 256, 1024
TT = SEQ // P
DEPTH = 2
RH, RQK, RV = 4, 256, 512
AH, AD = 8, 128
IH, ID = 8, 64
TOPK = min(256, SEQ // 4)
NG, EPG = 4, 8
NE = NG * EPG
FF = 512
KC = D // P
FC = FF // P
NB = 512
EPS = 1e-5
ALPHA = (2 * DEPTH) ** 0.25
IDX_SCALE = (ID ** -0.5) * (IH ** -0.5)
BIG = 1e30
TAKEN = -3e38
SLOTS = 64
PAIRS = NE // 2
RING = 6
TILE = KC * NB

SIZES = dict(rq=RH * RQK, rk=RH * RQK, rv=RH * RV, rg=RH * RV, aq=AH * AD, ak=AD, av=AD,
             iq=IH * ID, ik=ID, iw=IH, gr=D, ga=D)
COL = dict(zip(SIZES, np.cumsum([0, *SIZES.values()]).tolist()))

IN_TILES = [("ikw", COL["ik"], ID + IH), ("iq", COL["iq"], NB), ("ak", COL["ak"], 2 * AD)]
IN_TILES += [(f"{n}{i}", COL[n] + i * NB, NB) for n in ("aq", "rq", "rk", "rv", "rg", "gr", "ga")
             for i in range(SIZES[n] // NB)]
IN_TILE = {n: (c, w) for n, c, w in IN_TILES}
TILES = [n for n, _, _ in IN_TILES] + ["dsa0", "dsa1", "ret00", "ret01", "ret10", "ret11",
                                       "out0", "out1", "router"]
assert len(TILES) % RING == 0 and (6 * PAIRS) % RING == 0

JOBS = """XT0a XT1a Pikwv Piqv Tikwa Pakv Tiqa Paq0v Taka IX0v IX1v Paq1v Taq0a IX2v IX3v
Prq0v Taq1a Prq1v Trq0a Prk0v Trq1a Prk1v Trk0a Prv0a Trk1a AS0v Prv1a AT0a AS1v Prv2a AO0a AT1a
AS2v Prv3a AO1a AT2a AS3v Prg0a AO2a AT3a RS0v RS1v Prg1a AO3a Prg2a RY0v Prg3a RY1v Pgr0a RT0a
RY2v Pgr1a RT1a RY3v Pga0a RT2a Pga1a RT3a DO0v DO1v RO0v RO1v MT0a MT1a OUT0v OUT1v HT0a HT1a
RLv PCv""".split()
JOB = {j[:-1]: n for n, j in enumerate(JOBS)}
READER = {j[:-1]: j[-1] for j in JOBS}
GROUPS = 4

TABLES = dict(cos=TT * P, sin=TT * P, ident=P, before=P, ones=P, decay=RH * SEQ, causal=P + SEQ,
              iota=SLOTS, passes=4)
TAB = dict(zip(TABLES, np.cumsum([0, *TABLES.values()]).tolist()))
TAB_W = sum(TABLES.values())


def constant_table():
    f = np.float32
    t = np.zeros((P, TAB_W), f)

    def put(name, a):
        t[:, TAB[name]:TAB[name] + TABLES[name]] = a

    inv = (f(1) / (f(10000.0) ** (np.arange(0, RQK, 2, dtype=f) / f(RQK)))).astype(f)
    ang = np.arange(SEQ, dtype=f)[:, None] * inv[None, :]
    for name, fn in (("cos", np.cos), ("sin", np.sin)):
        put(name, fn(ang).astype(f).reshape(TT, P, P).transpose(1, 0, 2).reshape(P, -1))
    i = np.arange(P)
    put("ident", np.eye(P))
    put("before", i[:, None] < i[None, :])
    put("ones", 1)
    gamma = 1.0 - 2.0 ** (-5.0 - np.arange(RH))
    diff = np.arange(SEQ)[None, :] - i[:, None]
    decay = np.where(diff >= 0, gamma[:, None, None] ** np.maximum(diff, 0), 0) * RQK ** -0.5
    put("decay", decay.transpose(1, 0, 2).reshape(P, -1))
    hidden = np.concatenate([i[None, :] > i[:, None],
                             np.arange(SEQ)[None, :] > i[:, None] + P], axis=1)
    put("causal", np.where(hidden, -BIG, 0))
    put("iota", np.arange(SLOTS))
    put("passes", np.arange(4) * SLOTS)
    return t


def build(nc, x_in, w_in, w_ret_o, w_dsa_o, w_out, ln1_g, ln1_b, grp_w, grp_b, exp_w, exp_b,
          w_gate, w_up, w_down, ln2_g, ln2_b, tables, out):
    f32, bf16, i32, u32 = mybir.dt.float32, mybir.dt.bfloat16, mybir.dt.int32, mybir.dt.uint32
    ALU, ACT, X = mybir.AluOpType, mybir.ActivationFunctionType, mybir.AxisListType.X

    ctx = ExitStack()
    with ctx:
        def sb(name, shape, dt=f32):
            return ctx.enter_context(nc.sbuf_tensor(name, shape, dt))

        def sem(name):
            return ctx.enter_context(nc.semaphore(name))

        ring = sb("ring", [P, RING, TILE])
        tab = sb("tab", [P, TAB_W])
        x = sb("x", [P, TT, D])
        xT = sb("xT", [P, KC, SEQ])
        h = sb("h", [P, TT, D])
        qk = sb("qk", [P, RH, 4, SEQ])
        rv = sb("rv", [P, TT, RH * RV])
        rg = sb("rg", [P, RH, TT, RV])
        aqT = sb("aqT", [P, AH, SEQ])
        stage = sb("stage", [P, 2, TT, NB])
        tmp = sb("tmp", [P, TT, NB])
        sig = sb("sig", [P, TT, NB])
        akT = sb("akT", [P, SEQ])
        av = sb("av", [P, TT, AD])
        mask = sb("mask", [P, P + SEQ])
        wsc = sb("wsc", [P, TT, IH])
        rb = sb("rb", [P, NG + NE])
        m8 = sb("m8", [P, TT, 8])
        i8 = sb("i8", [P, TT, 8], u32)
        stat = sb("stat", [P, TT, 2, 6])
        mv = sb("mv", [P, TT, 2])
        var = sb("var", [P, TT])
        rstd = sb("rstd", [P, TT])
        nwt = sb("nwt", [P, TT])
        nmx = sb("nmx", [P, 4])
        ssum = sb("ssum", [P, 4])
        lg = sb("lg", [P, TT, NG + NE])
        g8 = sb("g8", [P, TT, 8])
        ml = sb("ml", [P, TT, NE])
        e4 = sb("e4", [P, TT, NG])
        gs = sb("gs", [P, TT, 12])
        oh = sb("oh", [P, TT, 2, NE])
        sel = sb("sel", [P, TT, NE])
        gate = sb("gate", [P, TT, NE])
        pos = sb("pos", [P, TT, NE])
        cnt = sb("cnt", [P, 6])
        npass = sb("npass", [P, 1], i32)

        def table(name, lo=0, hi=None):
            return tab[:, TAB[name] + lo:TAB[name] + (TABLES[name] if hi is None else hi)]

        ident = table("ident")
        iota = table("iota")
        causal = table("causal")

        rg_flat = rg[:, :, :, :].rearrange("p a t n -> p (a t n)")
        iqT = rg_flat[:, 0:1024].rearrange("p (b s) -> p b s", s=SEQ)
        ikT = rg_flat[:, 1024:1280]
        score = rg_flat[:, 1280:1280 + P + SEQ]
        prob = rg_flat[:, 1792:3328].rearrange("p (b a s) -> p b a s", b=2, a=2)
        pT = rg_flat[:, 3328:4096].rearrange("p (a s) -> p a s", a=2)
        stage_flat = stage[:, :, :, :].rearrange("p b t n -> p (b t n)")
        dT = stage_flat[:, 0:RH * (P + SEQ)].rearrange("p (a s) -> p a s", a=RH)
        lnp = stage_flat.rearrange("p (c n) -> p c n", c=2)
        retT = qk[:, :, :, :].rearrange("p a c s -> p (a c) s")
        mergedT = aqT
        ga = rv[:, :, 0:D]
        qk_flat = qk[:, :, :, :].rearrange("p a c s -> p (a c s)")
        xgT = qk_flat[:, 0:1024].rearrange("p (k s) -> p k s", k=KC)
        msig = qk_flat[:, 1024:1536]
        hid = qk_flat[:, 1536:2048]
        hidT = qk_flat[:, 2048:2560].rearrange("p (j s) -> p j s", j=FC)
        ytok = qk_flat[:, 2560:3584]
        gT = qk_flat[:, 3584:3840]
        aq_flat = aqT[:, :, :].rearrange("p a s -> p (a s)")
        pick = aq_flat[:, 0:256].rearrange("p (t s) -> p t s", t=TT)
        gpick = aq_flat[:, 256:512].rearrange("p (t s) -> p t s", t=TT)
        zeros = aq_flat[:, 512:512 + NB // 2].bitcast(bf16)

        psum = ctx.enter_context(nc.psum_tensor("psum", [P, 8, NB], f32))

        def banks(name):
            g = JOB[name] % GROUPS
            return psum[:, 2 * g:2 * g + 2, :]

        acc = psum[:, 0:4, :].rearrange("p (t n) c -> p t (n c)", t=TT)
        bank_g, bank_u = psum[:, 4, :], psum[:, 5, :]
        bank_y = [psum[:, 6, :], psum[:, 7, :]]
        wide_y = psum[:, 6:8, :].rearrange("p b c -> p (b c)")

        job_free = [sem(f"job_free{g}") for g in range(GROUPS)]
        full_a = [sem(f"full_a{g}") for g in range(GROUPS)]
        full_v = [sem(f"full_v{g}") for g in range(GROUPS)]
        tile_in = [sem(f"tile_in{s}") for s in range(RING)]
        tile_used = sem("tile_used")
        start_in = sem("start_in")
        x_ready = sem("x_ready")
        staged = sem("staged")
        dve_step = sem("dve_step")
        act_step = sem("act_step")
        max_ready = sem("max_ready")
        exp_ready = sem("exp_ready")
        p_ready = sem("p_ready")
        sig_ready = sem("sig_ready")
        sig_free = sem("sig_free")
        decayed = sem("decayed")
        yn_ready = sem("yn_ready")
        gates_in = sem("gates_in")
        merged_ready = sem("merged_ready")
        lnp_in = sem("lnp_in")
        rb_in = sem("rb_in")
        h_ready = sem("h_ready")
        router_max = sem("router_max")
        router_exp = sem("router_exp")
        sel_ready = sem("sel_ready")
        npass_pe, npass_act, npass_sp = sem("npass_pe"), sem("npass_act"), sem("npass_sp")
        picked, gpicked = sem("picked"), sem("gpicked")
        xg_full, xg_copied = sem("xg_full"), sem("xg_copied")
        gate_full, silu_in, up_full = sem("gate_full"), sem("silu_in"), sem("up_full")
        hid_ready = sem("hid_ready")
        hidT_full, hidT_copied = sem("hidT_full"), sem("hidT_copied")
        y_full = [sem(f"y_full{n}") for n in range(2)]
        y_copied = [sem(f"y_copied{n}") for n in range(2)]
        tg_full, tg_copied = sem("tg_full"), sem("tg_copied")
        acc_full = sem("acc_full")
        out_in = sem("out_in")

        block = ctx.enter_context(nc.Block())

        win_v = w_in.rearrange("l (p k) n -> l p k n", k=KC)
        ret_v = w_ret_o.rearrange("l (k p) n -> l p k n", p=P)
        dsa_v = w_dsa_o.rearrange("l (k p) n -> l p k n", p=P)
        out_v = w_out.rearrange("l (k p) n -> l p k n", p=P)
        grp_v = grp_w.rearrange("l (p k) n -> l p k n", k=KC)
        exp_v = exp_w.rearrange("l (p k) n -> l p k n", k=KC)
        gate_v = w_gate.rearrange("l e (p k) n -> (l e) p (k n)", k=KC)
        up_v = w_up.rearrange("l e (p k) n -> (l e) p (k n)", k=KC)
        down_v = w_down.rearrange("l e (j p) n -> (l e) p j n", p=P)

        def slot(i, w=NB):
            return ring[:, i % RING, 0:KC * w].rearrange("p (k n) -> p k n", k=KC)

        @block.sync
        def _(sp):
            def at(v, l):
                return v[bass.ds(l, 1)].rearrange("a p k n -> p (a k) n")

            def pair(e):
                for u, v in enumerate((gate_v, up_v)):
                    for n in range(2):
                        s = 2 * u + n
                        sp.wait_ge(tile_used, 1).then_inc(tile_used, -1)
                        sp.dma_start(ring[:, s, :], v[bass.ds(e + n, 1)].rearrange("a p n -> p (a n)")
                                     ).then_inc(tile_in[s], 16)
                for n in range(2):
                    sp.wait_ge(tile_used, 1).then_inc(tile_used, -1)
                    sp.dma_start(ring[:, 4 + n, :].rearrange("p (j n) -> p j n", j=FC),
                                 down_v[bass.ds(e + n, 1)].rearrange("a p j n -> p (a j) n")
                                 ).then_inc(tile_in[4 + n], 16)

            with sp.Fori(0, DEPTH) as l:
                for i, name in enumerate(TILES):
                    sp.wait_ge(tile_used, 1).then_inc(tile_used, -1)
                    landed = tile_in[i % RING]
                    if name in IN_TILE:
                        c, w = IN_TILE[name]
                        sp.dma_start(slot(i, w), at(win_v, l)[:, :, c:c + w]).then_inc(landed, 16)
                    elif name == "router":
                        sp.dma_start(slot(i, NG + NE)[:, :, 0:NG], at(grp_v, l)).then_inc(landed, 16)
                        sp.dma_start(slot(i, NG + NE)[:, :, NG:], at(exp_v, l)).then_inc(landed, 16)
                    else:
                        v = {"dsa": dsa_v, "ret": ret_v, "out": out_v}[name[:3]]
                        n = int(name[3])
                        k = KC * int(name[4]) if name[:3] == "ret" else 0
                        sp.dma_start(slot(i), at(v, l)[:, k:k + KC, n * NB:(n + 1) * NB]
                                     ).then_inc(landed, 16)
                pair(l * NE)
                sp.wait_ge(npass_sp, 1).then_inc(npass_sp, -1)
                passes = sp.value_load(npass[0:1, 0:1], min_val=1, max_val=SEQ // SLOTS)
                with sp.Fori(1, passes * PAIRS) as q:
                    pair(l * NE + (q % PAIRS) * 2)
            sp.wait_ge(x_ready, TT).then_inc(x_ready, -TT)
            sp.dma_start(out.rearrange("o (t p) n -> p (o t) n", p=P), x[:, :, :]
                         ).then_inc(out_in, 16)
            sp.wait_ge(out_in, 16)

        @block.tensor
        def _(pe):
            def begin(name):
                g = JOB[name] % GROUPS
                pe.wait_ge(job_free[g], 1).then_inc(job_free[g], -1)
                return psum[:, 2 * g:2 * g + 2, :]

            def finish(name, ins):
                full = full_a if READER[name] == "a" else full_v
                ins.then_inc(full[JOB[name] % GROUPS], 1)

            def copied(name, before):
                if JOB[before] - JOB[name] <= GROUPS:
                    pe.wait_ge(job_free[JOB[name] % GROUPS], 1)

            def product(name, lhs, tiles, w=NB):
                ps = begin(name)
                for n, (tile, lt) in enumerate(zip(tiles, lhs)):
                    i = TILES.index(tile)
                    need = 32 if tile == "router" else 16
                    pe.wait_ge(tile_in[i % RING], need).then_inc(tile_in[i % RING], -need)
                    for t in range(TT):
                        for k in range(KC):
                            mm = nc.tensor.matmul(ps[:, t, 0:w], lt[:, k, t * P:(t + 1) * P],
                                                  slot(i, w)[:, k, :],
                                                  start=(n == 0 and k == 0),
                                                  stop=(n == len(tiles) - 1 and k == KC - 1),
                                                  skip_group_check=len(tiles) > 1)
                            if t == 0 and k == 0:
                                mm.then_inc(tile_used, 1)
                finish(name, mm)

            def project(tile):
                product("P" + tile, [xT], [tile], IN_TILE[tile][1])

            def transposes(name, src, n=4):
                ps = begin(name)
                v = ps.rearrange("p b c -> p (b c)")
                for j in range(n):
                    for t in range(TT):
                        o = v[:, j * SEQ + t * P:j * SEQ + (t + 1) * P]
                        mm = nc.tensor.transpose(o, src(t, j), ident)
                finish(name, mm)

            def turn_rows(names, src, ready):
                views = [begin(name).rearrange("p b c -> p (b c)") for name in names]
                for t in range(TT):
                    pe.wait_ge(ready, 1).then_inc(ready, -1)
                    for i, name in enumerate(names):
                        for j in range(4):
                            mm = nc.tensor.transpose(
                                views[i][:, j * SEQ + t * P:j * SEQ + (t + 1) * P],
                                src[:, t, 4 * i + j:D:KC], ident)
                        if t == TT - 1:
                            finish(name, mm)

            def turn_stage(tile, b, n=4):
                pe.wait_ge(staged, 1).then_inc(staged, -1)
                transposes("T" + tile, lambda t, j: stage[:, b, t, j * P:(j + 1) * P], n)

            def index_scores(i):
                if i == 0:
                    copied("Tiq", "IX0")
                ps = begin(f"IX{i}")
                for a in range(2):
                    r = slice(a * ID, (a + 1) * ID)
                    for t in range(TT):
                        mm = nc.tensor.matmul(ps[:, a, t * P:P + t * SEQ], iqT[r, i, t * P:(t + 1) * P],
                                              ikT[r, 0:(t + 1) * P], start=True, stop=True)
                finish(f"IX{i}", mm)

            def attention_scores(i):
                ps = begin(f"AS{i}")
                for a in range(2):
                    for t in range(TT):
                        mm = nc.tensor.matmul(ps[:, a, t * P:t * P + (t + 1) * P],
                                              aqT[:, 2 * i + a, t * P:(t + 1) * P],
                                              akT[:, 0:(t + 1) * P], start=True, stop=True)
                finish(f"AS{i}", mm)

            def turn_probs(i):
                pe.wait_ge(p_ready, 1).then_inc(p_ready, -1)
                ps = begin(f"AT{i}")
                for a in range(2):
                    for b in range(3):
                        mm = nc.tensor.transpose(ps[:, a, b * P:(b + 1) * P],
                                                 prob[:, i % 2, a, b * P:(b + 1) * P], ident)
                finish(f"AT{i}", mm)

            def attend(i):
                copied(f"AT{i}", f"AO{i}")
                ps = begin(f"AO{i}").rearrange("p b c -> p (b c)")
                for a in range(2):
                    o = ps[:, a * SEQ:(a + 1) * SEQ]
                    nc.tensor.matmul(o[:, 0:P], av[:, 0, :], pT[:, a, 0:P], start=True, stop=True)
                    nc.tensor.matmul(o[:, P:SEQ], av[:, 0, :], pT[:, a, P:SEQ],
                                     start=True, stop=False)
                    mm = nc.tensor.matmul(o[:, P:SEQ], av[:, 1, :], pT[:, a, SEQ:SEQ + P],
                                          start=False, stop=True)
                finish(f"AO{i}", mm)

            def retention_scores(i):
                ps = begin(f"RS{i}")
                for a in range(2):
                    q = qk[:, 2 * i + a, 0:2, :]
                    k = qk[:, 2 * i + a, 2:4, :]
                    for m, (lo, hi) in enumerate(((0, SEQ), (SEQ, SEQ + P))):
                        for c in range(2):
                            mm = nc.tensor.matmul(ps[:, a, lo:hi], k[:, c, m * P:(m + 1) * P],
                                                  q[:, c, m * P:SEQ], start=(c == 0), stop=(c == 1))
                finish(f"RS{i}", mm)

            def retention_values(i):
                if i % 2 == 0:
                    pe.wait_ge(decayed, 1).then_inc(decayed, -1)
                ps = begin(f"RY{i}")
                v = rv[:, :, i * RV:(i + 1) * RV]
                nc.tensor.matmul(ps[:, 0, :], dT[:, i, 0:P], v[:, 0, :], start=True, stop=True)
                nc.tensor.matmul(ps[:, 1, :], dT[:, i, P:SEQ], v[:, 0, :], start=True, stop=False)
                mm = nc.tensor.matmul(ps[:, 1, :], dT[:, i, SEQ:SEQ + P], v[:, 1, :],
                                      start=False, stop=True)
                finish(f"RY{i}", mm)

            def turn_retention(i):
                pe.wait_ge(yn_ready, 1).then_inc(yn_ready, -1)
                transposes(f"RT{i}", lambda t, j: rg[:, i, t, j * P:(j + 1) * P])

            def gather():
                pe.wait_ge(picked, 1).then_inc(picked, -1)
                for k in range(KC):
                    for t in range(TT):
                        mm = nc.tensor.matmul(wide_y[:, k * P:(k + 1) * P], h[:, t, k:D:KC],
                                              pick[:, t, :], start=(t == 0), stop=(t == TT - 1))
                mm.then_inc(xg_full, 1)

            def pair_product(bank, lhs, chunks, s, lo, release):
                for k in range(chunks):
                    for e in range(2):
                        w = ring[:, s + e, :].rearrange("p (k n) -> p k n", k=chunks)
                        mm = nc.tensor.matmul(bank[e * SLOTS:(e + 1) * SLOTS, :],
                                              lhs[:, k, e * SLOTS:(e + 1) * SLOTS],
                                              w[:, k, lo:lo + NB], start=(k == 0),
                                              stop=(k == chunks - 1))
                        if k == 0 and e == 0 and release:
                            mm.then_inc(tile_used, release)
                return mm

            def arrived(s):
                for n in range(s, s + 2):
                    pe.wait_ge(tile_in[n], 16).then_inc(tile_in[n], -16)

            def combine(release=0):
                for t in range(TT):
                    for n in range(2):
                        mm = nc.tensor.matmul(acc[:, t, n * NB:(n + 1) * NB],
                                              gT[:, t * P:(t + 1) * P],
                                              ytok[:, n * NB:(n + 1) * NB], start=False,
                                              stop=False, skip_group_check=True)
                        if t == 0 and n == 0 and release:
                            mm.then_inc(tile_used, release)

            def outputs_copied():
                for n in range(2):
                    pe.wait_ge(y_copied[n], 1).then_inc(y_copied[n], -1)

            def experts(first, last):
                if first:
                    pe.wait_ge(xg_copied, 1).then_inc(xg_copied, -1)
                arrived(0)
                pair_product(bank_g, xgT, KC, 0, 0, 1 if first else 2).then_inc(gate_full, 1)
                if not first:
                    pe.wait_ge(tg_copied, 1).then_inc(tg_copied, -1)
                arrived(2)
                pair_product(bank_u, xgT, KC, 2, 0, 2).then_inc(up_full, 1)
                if not first:
                    outputs_copied()
                if not last:
                    gather()
                pe.wait_ge(hid_ready, 1).then_inc(hid_ready, -1)
                for j in range(FC):
                    mm = nc.tensor.transpose(bank_g[:, j * P:(j + 1) * P],
                                             hid[:, j * P:(j + 1) * P], ident)
                mm.then_inc(hidT_full, 1)
                if not first:
                    combine()
                pe.wait_ge(gpicked, 1).then_inc(gpicked, -1)
                for t in range(TT):
                    mm = nc.tensor.transpose(bank_u[:, t * P:(t + 1) * P], gpick[:, t, :], ident)
                mm.then_inc(tg_full, 1)
                pe.wait_ge(hidT_copied, 1).then_inc(hidT_copied, -1)
                if not last:
                    pe.wait_ge(xg_copied, 1).then_inc(xg_copied, -1)
                arrived(4)
                for n in range(2):
                    pair_product(bank_y[n], hidT, FC, 4, n * NB, 2 * (n == 0)
                                 ).then_inc(y_full[n], 1)

            with pe.Fori(0, DEPTH) as l:
                turn_rows(("XT0", "XT1"), x, x_ready)
                copied("XT0", "Pikw")
                copied("XT1", "Pikw")
                project("ikw")
                project("iq")
                turn_stage("ikw", 0, 1)
                project("ak")
                turn_stage("iq", 1)
                project("aq0")
                turn_stage("ak", 0, 1)
                index_scores(0)
                index_scores(1)
                project("aq1")
                turn_stage("aq0", 1)
                index_scores(2)
                index_scores(3)
                project("rq0")
                turn_stage("aq1", 0)
                project("rq1")
                turn_stage("rq0", 1)
                project("rk0")
                turn_stage("rq1", 0)
                project("rk1")
                turn_stage("rk0", 1)
                project("rv0")
                turn_stage("rk1", 0)
                attention_scores(0)
                project("rv1")
                turn_probs(0)
                attention_scores(1)
                project("rv2")
                attend(0)
                turn_probs(1)
                attention_scores(2)
                project("rv3")
                attend(1)
                turn_probs(2)
                attention_scores(3)
                project("rg0")
                attend(2)
                turn_probs(3)
                retention_scores(0)
                retention_scores(1)
                project("rg1")
                attend(3)
                project("rg2")
                retention_values(0)
                project("rg3")
                retention_values(1)
                project("gr0")
                turn_retention(0)
                retention_values(2)
                project("gr1")
                turn_retention(1)
                retention_values(3)
                project("ga0")
                turn_retention(2)
                project("ga1")
                turn_retention(3)
                product("DO0", [aqT], ["dsa0"])
                product("DO1", [aqT], ["dsa1"])
                copied("RT3", "RO0")
                for n in range(2):
                    product(f"RO{n}", [retT[:, 0:KC, :], retT[:, KC:, :]], [f"ret{n}0", f"ret{n}1"])
                for i in range(2):
                    pe.wait_ge(merged_ready, 1).then_inc(merged_ready, -1)
                    transposes(f"MT{i}", lambda t, j: h[:, t, (4 * i + j) * P:(4 * i + j + 1) * P])
                copied("MT0", "OUT0")
                copied("MT1", "OUT0")
                for n in range(2):
                    product(f"OUT{n}", [mergedT], [f"out{n}"])
                turn_rows(("HT0", "HT1"), h, h_ready)
                copied("HT0", "RL")
                copied("HT1", "RL")
                product("RL", [xT], ["router"], NG + NE)
                pe.wait_ge(sel_ready, 1).then_inc(sel_ready, -1)
                ps = begin("PC")
                nc.tensor.matmul(ps[:, 0, 0:NE], table("before"), sel[:, 0, :], start=True, stop=True)
                for c, m in ((1, "before"), (2, "ones")):
                    nc.tensor.matmul(ps[:, 0, c * NE:(c + 1) * NE], table("ones"), sel[:, 0, :],
                                     start=True, stop=False)
                    mm = nc.tensor.matmul(ps[:, 0, c * NE:(c + 1) * NE], table(m), sel[:, 1, :],
                                          start=False, stop=True)
                finish("PC", mm)
                for g in range(GROUPS):
                    pe.wait_ge(job_free[g], 1)
                pe.wait_ge(npass_pe, 1).then_inc(npass_pe, -1)
                for b in range(4):
                    nc.tensor.matmul(psum[:, b, :], zeros[:, 0:P], zeros, start=True,
                                     stop=False, skip_group_check=True)
                passes = pe.value_load(npass[0:1, 0:1], min_val=1, max_val=SEQ // SLOTS)
                with pe.Fori(0, passes) as _p:
                    gather()
                    experts(True, False)
                    with pe.Fori(1, PAIRS - 1) as _j:
                        experts(False, False)
                    experts(False, True)
                    outputs_copied()
                    pe.wait_ge(tg_copied, 1).then_inc(tg_copied, -1)
                    combine(1)
                for b in range(4):
                    mm = nc.tensor.matmul(psum[:, b, :], zeros[:, 0:P], zeros, start=False,
                                          stop=True, skip_group_check=True)
                mm.then_inc(acc_full, 1)

        @block.scalar
        def _(act):
            def take(name):
                g = JOB[name] % GROUPS
                act.wait_ge(full_a[g], 1).then_inc(full_a[g], -1)
                return psum[:, 2 * g:2 * g + 2, :]

            def copy_out(name, dst, n=1024):
                src = take(name).rearrange("p b c -> p (b c)")[:, 0:n]
                if len(dst.shape) == 3:
                    src = src.rearrange("p (a b) -> p a b", a=dst.shape[1])
                elif len(dst.shape) == 4:
                    src = src.rearrange("p (a b c) -> p a b c", a=dst.shape[1], b=dst.shape[2])
                nc.scalar.activation(dst, src, ACT.Copy).then_inc(job_free[JOB[name] % GROUPS], 1)

            def exps(i):
                act.wait_ge(max_ready, 1).then_inc(max_ready, -1)
                for a in range(2):
                    for t in range(TT):
                        v = prob[:, i % 2, a, t * P:P + t * SEQ]
                        e = nc.scalar.activation(v, v, ACT.Exp, bias=nmx[:, 2 * t + a:2 * t + a + 1],
                                                 accum_out=ssum[:, 2 * t + a:2 * t + a + 1])
                        if (a, t) != (1, TT - 1):
                            e.then_inc(act_step, 1)
                            act.wait_ge(act_step, 1).then_inc(act_step, -1)
                e.then_inc(exp_ready, 1)

            def silu_gate(n):
                ps = take(f"Prg{n}")
                act.wait_ge(sig_free, 1).then_inc(sig_free, -1)
                nc.scalar.activation(sig[:, :, :], ps, ACT.Sigmoid).then_inc(sig_ready, 1)

            def branch_gate(name, dst):
                ps = take("P" + name)
                g = JOB["P" + name] % GROUPS
                nc.scalar.activation(dst, ps, ACT.Sigmoid).then_inc(act_step, 1)
                act.wait_ge(act_step, 1).then_inc(act_step, -1)
                act.sem_inc(job_free[g], 1)
                act.sem_inc(gates_in, 1)

            def experts():
                act.wait_ge(gate_full, 1).then_inc(gate_full, -1)
                nc.scalar.activation(msig, bank_g, ACT.Sigmoid).then_inc(silu_in, 1)
                act.wait_ge(hidT_full, 1).then_inc(hidT_full, -1)
                nc.scalar.activation(hidT, bank_g.rearrange("p (j s) -> p j s", j=FC), ACT.Copy
                                     ).then_inc(hidT_copied, 1)
                act.wait_ge(tg_full, 1).then_inc(tg_full, -1)
                nc.scalar.activation(gT, bank_u[:, 0:SEQ], ACT.Copy).then_inc(tg_copied, 1)
                for n in range(2):
                    act.wait_ge(y_full[n], 1).then_inc(y_full[n], -1)
                    nc.scalar.activation(ytok[:, n * NB:(n + 1) * NB], bank_y[n], ACT.Copy
                                         ).then_inc(y_copied[n], 1)

            def ln_params(g, b, l):
                for n, v in enumerate((g, b)):
                    act.dma_start(lnp[:, n, :], v[bass.ds(l, 1)].broadcast_to((P, D))
                                  ).then_inc(lnp_in, 16)

            act.dma_start(x[:, :, :], x_in.rearrange("o (t p) n -> p (o t) n", p=P)
                          ).then_inc(start_in, 16)
            act.dma_start(tab[:, :], tables).then_inc(start_in, 16)
            with act.Fori(0, DEPTH) as l:
                act.dma_start(rb[:, 0:NG], grp_b[bass.ds(l, 1)].broadcast_to((P, NG))
                              ).then_inc(rb_in, 16)
                act.dma_start(rb[:, NG:], exp_b[bass.ds(l, 1)].broadcast_to((P, NE))
                              ).then_inc(rb_in, 16)
                copy_out("XT0", xT[:, 0:4, :])
                copy_out("XT1", xT[:, 4:8, :])
                copy_out("Tikw", ikT, SEQ)
                copy_out("Tiq", iqT)
                copy_out("Tak", akT[:, :], SEQ)
                copy_out("Taq0", aqT[:, 0:4, :])
                copy_out("Taq1", aqT[:, 4:8, :])
                copy_out("Trq0", qk[:, 0:2, 0:2, :])
                copy_out("Trq1", qk[:, 2:4, 0:2, :])
                copy_out("Trk0", qk[:, 0:2, 2:4, :])
                copy_out("Prv0", rv[:, :, 0:NB])
                copy_out("Trk1", qk[:, 2:4, 2:4, :])
                exps(0)
                for i in range(1, 4):
                    copy_out(f"Prv{i}", rv[:, :, i * NB:(i + 1) * NB])
                    if i >= 2:
                        copy_out(f"AO{i - 2}", aqT[:, 2 * i - 4:2 * i - 2, :], 2 * SEQ)
                    turned = take(f"AT{i - 1}")
                    nc.scalar.activation(pT[:, :, :], turned[:, :, 0:P + SEQ], ACT.Copy
                                         ).then_inc(job_free[JOB[f"AT{i - 1}"] % GROUPS], 1)
                    exps(i)
                silu_gate(0)
                copy_out("AO2", aqT[:, 4:6, :], 2 * SEQ)
                turned = take("AT3")
                nc.scalar.activation(pT[:, :, :], turned[:, :, 0:P + SEQ], ACT.Copy
                                     ).then_inc(job_free[JOB["AT3"] % GROUPS], 1)
                silu_gate(1)
                copy_out("AO3", aqT[:, 6:8, :], 2 * SEQ)
                silu_gate(2)
                silu_gate(3)
                branch_gate("gr0", h[:, :, 0:NB])
                copy_out("RT0", retT[:, 0:4, :])
                branch_gate("gr1", h[:, :, NB:D])
                copy_out("RT1", retT[:, 4:8, :])
                branch_gate("ga0", ga[:, :, 0:NB])
                copy_out("RT2", retT[:, 8:12, :])
                branch_gate("ga1", ga[:, :, NB:D])
                copy_out("RT3", retT[:, 12:16, :])
                ln_params(ln1_g, ln1_b, l)
                for i in range(2):
                    copy_out(f"MT{i}", mergedT[:, 4 * i:4 * i + 4, :])
                for i in range(2):
                    copy_out(f"HT{i}", xT[:, 4 * i:4 * i + 4, :])
                act.wait_ge(router_max, 1).then_inc(router_max, -1)
                ln_params(ln2_g, ln2_b, l)
                for t in range(TT):
                    nc.scalar.activation(e4[:, t, :], lg[:, t, 0:NG], ACT.Exp,
                                         bias=gs[:, t, 0:1], accum_out=gs[:, t, 1:2]
                                         ).then_inc(act_step, 1)
                    act.wait_ge(act_step, 1).then_inc(act_step, -1)
                nc.scalar.activation(gs[:, :, 3:4], gs[:, :, 2:3], ACT.Exp).then_inc(router_exp, 1)
                act.wait_ge(npass_act, 1).then_inc(npass_act, -1)
                passes = act.value_load(npass[0:1, 0:1], min_val=1, max_val=SEQ // SLOTS)
                with act.Fori(0, passes * PAIRS) as _q:
                    experts()

        @block.vector
        def _(dve):
            V = nc.vector

            def step(ins):
                ins.then_inc(dve_step, 1)
                dve.wait_ge(dve_step, 1).then_inc(dve_step, -1)

            def take(name):
                g = JOB[name] % GROUPS
                dve.wait_ge(full_v[g], 1).then_inc(full_v[g], -1)
                return psum[:, 2 * g:2 * g + 2, :]

            def free(name):
                dve.sem_inc(job_free[JOB[name] % GROUPS], 1)

            def rotate(name, b, half, heads):
                ps = take(name)
                w = 2 * half * heads
                for t in range(TT):
                    src = ps[:, t, 0:w].rearrange("p (a d) -> p a d", d=half)
                    for fn, dst in (("cos", tmp), ("sin", sig)):
                        f = table(fn, t * P, (t + 1) * P)[:, 0:P:P // half]
                        step(V.tensor_tensor(dst[:, t, 0:w].rearrange("p (a d) -> p a d", d=half),
                                             src, f.unsqueeze(1).broadcast_to((P, 2 * heads, half)),
                                             ALU.mult))
                for t in range(TT):
                    def halves(a):
                        v = a.rearrange("p (a c d) -> p a c d", c=2, d=half)
                        return v[:, :, 0, :], v[:, :, 1, :]
                    (c1, c2), (s1, s2) = halves(tmp[:, t, 0:w]), halves(sig[:, t, 0:w])
                    o1, o2 = halves(stage[:, b, t, 0:w])
                    V.tensor_tensor(o1, c1, s2, ALU.subtract)
                    step(V.tensor_tensor(o2, c2, s1, ALU.add))
                return ps

            def norm_stats(n):
                for t in range(TT):
                    last = V.bn_aggr(mv[:, t, :], stat[:, t, 0:n, :].rearrange("p a b -> p (a b)"))
                step(last)
                step(V.tensor_scalar(var[:, :], mv[:, :, 1], EPS, None, ALU.add))
                step(V.tensor_scalar(rstd[:, :].bitcast(i32), var[:, :].bitcast(i32), 1, None,
                                     ALU.logical_shift_right))
                step(V.tensor_scalar(rstd[:, :].bitcast(i32), rstd[:, :].bitcast(i32), -1.0,
                                     float(0x5F3759DF), ALU.mult, ALU.add))
                for _ in range(3):
                    step(V.tensor_tensor(nwt[:, :], rstd[:, :], rstd[:, :], ALU.mult))
                    step(V.scalar_tensor_tensor(out=nwt[:, :], in0=nwt[:, :], scalar=-0.5,
                                                in1=var[:, :], op0=ALU.mult, op1=ALU.mult))
                    step(V.scalar_tensor_tensor(out=rstd[:, :], in0=nwt[:, :], scalar=1.5,
                                                in1=rstd[:, :], op0=ALU.add, op1=ALU.mult))

            def halves_stats(src, n):
                for t in range(TT):
                    last = V.bn_stats(stat[:, t, n, :], src[:, t, n * NB:(n + 1) * NB])
                step(last)

            def layer_norm(src, dst, done):
                norm_stats(2)
                step(V.tensor_scalar(mv[:, :, 0], mv[:, :, 0], -1.0, None, ALU.mult))
                dve.wait_ge(lnp_in, 32).then_inc(lnp_in, -32)
                for t in range(TT):
                    step(V.scalar_tensor_tensor(out=dst[:, t, :], in0=src[:, t, :],
                                                scalar=mv[:, t, 0:1], in1=lnp[:, 0, :],
                                                op0=ALU.add, op1=ALU.mult))
                    V.scalar_tensor_tensor(out=dst[:, t, :], in0=dst[:, t, :],
                                           scalar=rstd[:, t:t + 1], in1=lnp[:, 1, :],
                                           op0=ALU.mult, op1=ALU.add).then_inc(done, 1)

            def index_scores(i):
                ps = take(f"IX{i}")
                for a in range(2):
                    hd = 2 * i + a
                    for t in range(TT):
                        lo, hi = t * P, P + t * SEQ
                        step(V.tensor_scalar(tmp[:, 0, lo:hi], ps[:, a, lo:hi], 0.0,
                                             wsc[:, t, hd:hd + 1], ALU.max, ALU.mult))
                    if a == 1:
                        free(f"IX{i}")
                    prev = causal if hd == 0 else score
                    step(V.tensor_tensor(score, prev, tmp[:, 0, 0:P + SEQ], ALU.add))

            def select():
                for lo, hi in ((0, P), (P, P + SEQ)):
                    for _ in range(TOPK // 8):
                        step(V.max(m8[:, 0, :], score[:, lo:hi]))
                        step(V.match_replace(score[:, lo:hi], m8[:, 0, :], score[:, lo:hi], TAKEN))
                step(V.tensor_scalar(score, score, TAKEN, 1.0, ALU.is_equal, ALU.subtract))
                step(V.scalar_tensor_tensor(out=mask[:, :], in0=score, scalar=BIG, in1=causal,
                                            op0=ALU.mult, op1=ALU.min))

            def softmax(i):
                ps = take(f"AS{i}")
                pr = prob[:, i % 2, :, :]
                for a in range(2):
                    step(V.scalar_tensor_tensor(out=pr[:, a, :], in0=ps[:, a, 0:P + SEQ],
                                                scalar=AD ** -0.5, in1=mask[:, :],
                                                op0=ALU.mult, op1=ALU.add))
                free(f"AS{i}")
                for t in range(TT):
                    step(V.tensor_reduce(nmx[:, 2 * t:2 * t + 2], pr[:, :, t * P:P + t * SEQ], X,
                                         ALU.max))
                step(V.tensor_scalar(nmx[:, :], nmx[:, :], -1.0, None, ALU.mult))
                dve.sem_inc(max_ready, 1)
                dve.wait_ge(exp_ready, 1).then_inc(exp_ready, -1)
                step(V.reciprocal(ssum[:, :], ssum[:, :]))
                for a in range(2):
                    for t in range(TT):
                        v = pr[:, a, t * P:P + t * SEQ]
                        step(V.tensor_scalar(v, v, ssum[:, 2 * t + a:2 * t + a + 1], None, ALU.mult))
                dve.sem_inc(p_ready, 1)

            def silu(n):
                dve.wait_ge(sig_ready, 1).then_inc(sig_ready, -1)
                step(V.tensor_tensor(rg[:, n, :, :], banks(f"Prg{n}"), sig[:, :, :], ALU.mult))
                free(f"Prg{n}")
                dve.sem_inc(sig_free, 1)

            def decay(i):
                ps = take(f"RS{i}")
                for a in range(2):
                    hd = 2 * i + a
                    d = table("decay", hd * SEQ, (hd + 1) * SEQ)
                    step(V.tensor_tensor(dT[:, hd, 0:SEQ], ps[:, a, 0:SEQ], d, ALU.mult))
                    step(V.tensor_tensor(dT[:, hd, SEQ:SEQ + P], ps[:, a, SEQ:SEQ + P], d[:, 0:P],
                                         ALU.mult))
                free(f"RS{i}")
                dve.sem_inc(decayed, 1)

            def group_norm(i):
                ps = take(f"RY{i}")
                for t in range(TT):
                    step(V.bn_stats(stat[:, t, 0, :], ps[:, t, :]))
                norm_stats(1)
                for t in range(TT):
                    step(V.tensor_scalar(tmp[:, t, :], ps[:, t, :], mv[:, t, 0:1],
                                         rstd[:, t:t + 1], ALU.subtract, ALU.mult))
                free(f"RY{i}")
                step(V.tensor_tensor(rg[:, i, :, :], rg[:, i, :, :], tmp[:, :, :], ALU.mult))
                dve.sem_inc(yn_ready, 1)

            def best(v):
                for t in range(TT):
                    last = V.max(m8[:, t, :], v[:, t, :])
                step(last)
                for t in range(TT):
                    last = V.max_index(i8[:, t, :], m8[:, t, :], v[:, t, :])
                step(last)

            def router():
                ps = take("RL")
                dve.wait_ge(rb_in, 32).then_inc(rb_in, -32)
                for t in range(TT):
                    step(V.tensor_tensor(lg[:, t, :], ps[:, t, 0:NG + NE], rb[:, :], ALU.add))
                free("RL")
                step(V.tensor_copy(g8[:, :, 0:NG], lg[:, :, 0:NG]))
                best(g8)
                V.tensor_scalar(gs[:, :, 0:1], m8[:, :, 0:1], -1.0, None, ALU.mult)
                step(V.tensor_copy(gs[:, :, 4:5], i8[:, :, 0:1]))
                step(V.tensor_tensor(oh[:, :, 0, 0:NG],
                                     iota[:, 0:NG].unsqueeze(1).broadcast_to((P, TT, NG)),
                                     gs[:, :, 4:5].broadcast_to((P, TT, NG)), ALU.is_equal))
                step(V.tensor_scalar(oh[:, :, 0, 0:NG], oh[:, :, 0, 0:NG], 1.0, BIG,
                                     ALU.subtract, ALU.mult))
                for t in range(TT):
                    last = V.tensor_tensor(
                        ml[:, t, :].rearrange("p (g e) -> p g e", g=NG),
                        lg[:, t, NG:].rearrange("p (g e) -> p g e", g=NG),
                        oh[:, t, 0, 0:NG].unsqueeze(2).broadcast_to((P, NG, EPG)), ALU.add)
                step(last)
                best(ml)
                V.tensor_tensor(gs[:, :, 2:3], m8[:, :, 1:2], m8[:, :, 0:1], ALU.subtract)
                step(V.tensor_copy(gs[:, :, 5:7], i8[:, :, 0:2]))
                for c in range(2):
                    for t in range(TT):
                        last = V.tensor_scalar(oh[:, t, c, :], iota[:, 0:NE], gs[:, t, 5 + c:6 + c],
                                               None, ALU.is_equal)
                step(last)
                step(V.tensor_tensor(sel[:, :, :], oh[:, :, 0, :], oh[:, :, 1, :], ALU.add))
                dve.sem_inc(router_max, 1)
                dve.sem_inc(sel_ready, 1)
                dve.wait_ge(router_exp, 1).then_inc(router_exp, -1)
                step(V.tensor_scalar(gs[:, :, 7:8], gs[:, :, 3:4], 1.0, None, ALU.add))
                step(V.tensor_tensor(gs[:, :, 7:8], gs[:, :, 7:8], gs[:, :, 1:2], ALU.mult))
                step(V.reciprocal(gs[:, :, 7:8], gs[:, :, 7:8]))
                step(V.tensor_tensor(gs[:, :, 8:9], gs[:, :, 7:8], gs[:, :, 3:4], ALU.mult))
                for t in range(TT):
                    step(V.tensor_scalar(gate[:, t, :], oh[:, t, 0, :], gs[:, t, 7:8], None,
                                         ALU.mult))
                    step(V.scalar_tensor_tensor(out=gate[:, t, :], in0=oh[:, t, 1, :],
                                                scalar=gs[:, t, 8:9], in1=gate[:, t, :],
                                                op0=ALU.mult, op1=ALU.add))

            def places():
                ps = take("PC")
                pc = ps[:, 0, 0:3 * NE].rearrange("p (c e) -> p c e", c=3)
                for t in range(TT):
                    step(V.scalar_tensor_tensor(out=pos[:, t, :], in0=pc[:, t, :], scalar=1.0,
                                                in1=sel[:, t, :], op0=ALU.add, op1=ALU.mult))
                step(V.tensor_scalar(pos[:, :, :], pos[:, :, :], -1.0, None, ALU.add))
                step(V.tensor_reduce(cnt[:, 0:1], pc[:, 2, :], X, ALU.max))
                free("PC")
                step(V.tensor_scalar(cnt[:, 1:5], table("passes"), cnt[:, 0:1], None, ALU.is_lt))
                step(V.tensor_reduce(cnt[:, 5:6], cnt[:, 1:5], X, ALU.add))
                step(V.tensor_copy(npass[:, :], cnt[:, 5:6]))
                step(V.memset(zeros, 0.0))
                dve.sem_inc(npass_sp, 1)
                dve.sem_inc(npass_pe, 1)
                dve.sem_inc(npass_act, 1)

            def lists(e0):
                for e in range(2):
                    for t in range(TT):
                        step(V.tensor_scalar(pick[:, t, e * SLOTS:(e + 1) * SLOTS], iota,
                                             pos[:, t, bass.ds(e0 + e, 1)], None, ALU.is_equal))
                dve.sem_inc(picked, 1)

            def gathered():
                dve.wait_ge(xg_full, 1).then_inc(xg_full, -1)
                V.tensor_copy(xgT, wide_y.rearrange("p (k s) -> p k s", k=KC)
                              ).then_inc(xg_copied, 1)

            def experts(e0, last):
                dve.wait_ge(silu_in, 1).then_inc(silu_in, -1)
                step(V.tensor_tensor(msig, bank_g, msig, ALU.mult))
                for e in range(2):
                    for t in range(TT):
                        c = slice(e * SLOTS, (e + 1) * SLOTS)
                        step(V.tensor_scalar(gpick[:, t, c], pick[:, t, c],
                                             gate[:, t, bass.ds(e0 + e, 1)], None, ALU.mult))
                dve.sem_inc(gpicked, 1)
                if not last:
                    lists(e0 + 2)
                dve.wait_ge(up_full, 1).then_inc(up_full, -1)
                V.tensor_tensor(hid, msig, bank_u, ALU.mult).then_inc(hid_ready, 1)
                if not last:
                    gathered()

            step(V.memset(g8[:, :, :], -BIG))
            for g in range(GROUPS):
                dve.sem_inc(job_free[g], 1)
            dve.sem_inc(tile_used, RING - 1)
            dve.sem_inc(sig_free, 1)
            dve.wait_ge(start_in, 32)
            dve.sem_inc(x_ready, TT)
            with dve.Fori(0, DEPTH) as l:
                ps = rotate("Pikw", 0, ID // 2, 1)
                for t in range(TT):
                    step(V.tensor_copy(stage[:, 0, t, ID:2 * ID], stage[:, 0, t, 0:ID]))
                step(V.tensor_scalar(wsc[:, :, :], ps[:, :, ID:ID + IH], IDX_SCALE, None, ALU.mult))
                free("Pikw")
                dve.sem_inc(staged, 1)
                rotate("Piq", 1, ID // 2, IH)
                free("Piq")
                dve.sem_inc(staged, 1)
                ps = rotate("Pak", 0, AD // 2, 1)
                step(V.tensor_copy(av[:, :, :], ps[:, :, AD:2 * AD]))
                free("Pak")
                dve.sem_inc(staged, 1)
                rotate("Paq0", 1, AD // 2, 4)
                free("Paq0")
                dve.sem_inc(staged, 1)
                index_scores(0)
                index_scores(1)
                rotate("Paq1", 0, AD // 2, 4)
                free("Paq1")
                dve.sem_inc(staged, 1)
                index_scores(2)
                index_scores(3)
                for n, name in enumerate(("rq0", "rq1", "rk0", "rk1")):
                    rotate("P" + name, (n + 1) % 2, RQK // 2, 2)
                    free("P" + name)
                    dve.sem_inc(staged, 1)
                    if n == 2:
                        select()
                for i in range(4):
                    softmax(i)
                silu(0)
                decay(0)
                decay(1)
                silu(1)
                silu(2)
                group_norm(0)
                silu(3)
                for i in range(1, RH):
                    group_norm(i)
                dve.wait_ge(gates_in, 4).then_inc(gates_in, -4)
                for n in range(2):
                    ps = take(f"DO{n}")
                    c = slice(n * NB, (n + 1) * NB)
                    step(V.tensor_tensor(ga[:, :, c], ga[:, :, c], ps, ALU.mult))
                    free(f"DO{n}")
                for n in range(2):
                    ps = take(f"RO{n}")
                    c = slice(n * NB, (n + 1) * NB)
                    step(V.tensor_tensor(h[:, :, c], h[:, :, c], ps, ALU.mult))
                    free(f"RO{n}")
                    step(V.tensor_tensor(h[:, :, c], h[:, :, c], ga[:, :, c], ALU.add))
                    dve.sem_inc(merged_ready, 1)
                for n in range(2):
                    ps = take(f"OUT{n}")
                    c = slice(n * NB, (n + 1) * NB)
                    step(V.scalar_tensor_tensor(out=x[:, :, c], in0=x[:, :, c], scalar=ALPHA,
                                                in1=ps, op0=ALU.mult, op1=ALU.add))
                    free(f"OUT{n}")
                    halves_stats(x, n)
                layer_norm(x, h, h_ready)
                router()
                places()
                passes = dve.value_load(npass[0:1, 0:1], min_val=1, max_val=SEQ // SLOTS)
                with dve.Fori(0, passes) as _p:
                    lists(0)
                    gathered()
                    with dve.Fori(0, PAIRS - 1) as j:
                        experts(j * 2, False)
                    experts(NE - 2, True)
                    step(V.tensor_scalar(pos[:, :, :], pos[:, :, :], -float(SLOTS), None, ALU.add))
                dve.wait_ge(acc_full, 1).then_inc(acc_full, -1)
                for t in range(TT):
                    step(V.scalar_tensor_tensor(out=x[:, t, :], in0=h[:, t, :], scalar=ALPHA,
                                                in1=acc[:, t, :], op0=ALU.mult, op1=ALU.add))
                for n in range(2):
                    halves_stats(x, n)
                layer_norm(x, x, x_ready)


_INS = ['x', 'w_in', 'w_ret_o', 'w_dsa_o', 'w_out', 'ln1_g', 'ln1_b', 'router_grp_w',
        'router_grp_b', 'router_exp_w', 'router_exp_b', 'w_gate', 'w_up', 'w_down', 'ln2_g',
        'ln2_b']


def kernel(**inputs):
    import concourse.bacc as _bacc
    from concourse.bass_utils import run_bass_kernel_spmd as _run

    nc = _bacc.Bacc("TRN2", target_bir_lowering=False, num_devices=1)
    arrays, args = {}, []
    given = {n: np.ascontiguousarray(inputs[n]) for n in _INS}
    for name, a in [*given.items(), ("tables", constant_table())]:
        arrays[f"in_{name}_dram"] = a
        args.append(nc.dram_tensor(f"in_{name}_dram", a.shape, mybir.dt.from_np(a.dtype),
                                   kind="ExternalInput").ap())
    args.append(nc.dram_tensor("out_0_dram", (1, SEQ, D), mybir.dt.float32,
                               kind="ExternalOutput").ap())
    build(nc, *args)
    r = _run(nc, [arrays], core_ids=[0])
    return r.results[0]["out_0_dram"]
```

```python
import numpy as np
import concourse.bass as bass
from concourse import mybir
from contextlib import ExitStack

P = 128
SEQ, D = 256, 1024
TT = SEQ // P
DEPTH = 2
RH, RQK, RV = 4, 256, 512
AH, AD = 8, 128
IH, ID = 8, 64
TOPK = min(256, SEQ // 4)
NG, EPG = 4, 8
NE = NG * EPG
FF = 512
KC = D // P
FC = FF // P
NB = 512
EPS = 1e-5
ALPHA = (2 * DEPTH) ** 0.25
IDX_SCALE = (ID ** -0.5) * (IH ** -0.5)
BIG = 1e30
TAKEN = -3e38
SLOTS = 64
PAIRS = NE // 2
RING = 6
TILE = KC * NB

SIZES = dict(rq=RH * RQK, rk=RH * RQK, rv=RH * RV, rg=RH * RV, aq=AH * AD, ak=AD, av=AD,
             iq=IH * ID, ik=ID, iw=IH, gr=D, ga=D)
COL = dict(zip(SIZES, np.cumsum([0, *SIZES.values()]).tolist()))

IN_TILES = [("ikw", COL["ik"], ID + IH), ("iq", COL["iq"], NB), ("ak", COL["ak"], 2 * AD)]
IN_TILES += [(f"{n}{i}", COL[n] + i * NB, NB) for n in ("aq", "rq", "rk", "rv", "rg", "gr", "ga")
             for i in range(SIZES[n] // NB)]
IN_TILE = {n: (i, c, w) for i, (n, c, w) in enumerate(IN_TILES)}
TILES = ["dsa0", "dsa1", "ret00", "ret01", "ret10", "ret11", "out0", "out1", "router"]
RAW, HIGH = 3, 2
assert len(IN_TILES) % RAW == 0 and RAW + HIGH + 1 == RING and 6 * PAIRS % RING == 0
OUTSIDE = 3
assert (len(TILES) + 6 - OUTSIDE) % RING == 0

JOBS = """XT0a XT1a Pikwv Piqv Tikwa Pakv Tiqa Paq0v Taka IX0v IX1v Paq1v Taq0a IX2v IX3v
Prq0v Taq1a Prq1v Trq0a Prk0v Trq1a Prk1v Trk0a Prv0a Trk1a AS0v Prv1a AT0a AS1v Prv2a AO0a AT1a
AS2v Prv3a AO1a AT2a AS3v Prg0a AO2a AT3a RS0v RS1v Prg1a AO3a Prg2a RY0v Prg3a RY1v Pgr0a RT0a
RY2v Pgr1a RT1a RY3v Pga0a RT2a Pga1a RT3a DO0v DO1v RO0v RO1v MT0a MT1a OUT0v OUT1v HT0a HT1a
RLv PCv""".split()
JOB = {j[:-1]: n for n, j in enumerate(JOBS)}
READER = {j[:-1]: j[-1] for j in JOBS}
GROUPS = 4

TABLES = dict(cos=TT * P, sin=TT * P, ident=P, before=P, ones=P, decay=RH * SEQ, causal=P + SEQ,
              iota=SLOTS, passes=4)
TAB = dict(zip(TABLES, np.cumsum([0, *TABLES.values()]).tolist()))
TAB_W = sum(TABLES.values())


def constant_table():
    f = np.float32
    t = np.zeros((P, TAB_W), f)

    def put(name, a):
        t[:, TAB[name]:TAB[name] + TABLES[name]] = a

    inv = (f(1) / (f(10000.0) ** (np.arange(0, RQK, 2, dtype=f) / f(RQK)))).astype(f)
    ang = np.arange(SEQ, dtype=f)[:, None] * inv[None, :]
    for name, fn in (("cos", np.cos), ("sin", np.sin)):
        put(name, fn(ang).astype(f).reshape(TT, P, P).transpose(1, 0, 2).reshape(P, -1))
    i = np.arange(P)
    put("ident", np.eye(P))
    put("before", i[:, None] < i[None, :])
    put("ones", 1)
    gamma = 1.0 - 2.0 ** (-5.0 - np.arange(RH))
    diff = np.arange(SEQ)[None, :] - i[:, None]
    decay = np.where(diff >= 0, gamma[:, None, None] ** np.maximum(diff, 0), 0) * RQK ** -0.5
    put("decay", decay.transpose(1, 0, 2).reshape(P, -1))
    hidden = np.concatenate([i[None, :] > i[:, None],
                             np.arange(SEQ)[None, :] > i[:, None] + P], axis=1)
    put("causal", np.where(hidden, -BIG, 0))
    put("iota", np.arange(SLOTS))
    put("passes", np.arange(4) * SLOTS)
    return t


def build(nc, x_in, w_in, w_ret_o, w_dsa_o, w_out, ln1_g, ln1_b, grp_w, grp_b, exp_w, exp_b,
          w_gate, w_up, w_down, ln2_g, ln2_b, tables, out):
    f32, bf16, i32, u32 = mybir.dt.float32, mybir.dt.bfloat16, mybir.dt.int32, mybir.dt.uint32
    f32r = mybir.dt.float32r
    ALU, ACT, X = mybir.AluOpType, mybir.ActivationFunctionType, mybir.AxisListType.X

    ctx = ExitStack()
    with ctx:
        def sb(name, shape, dt=f32):
            return ctx.enter_context(nc.sbuf_tensor(name, shape, dt))

        def sem(name):
            return ctx.enter_context(nc.semaphore(name))

        ring = sb("ring", [P, RING, TILE])
        tab = sb("tab", [P, TAB_W])
        x_xT = sb("x_xT", [P, 2 * TT * D])
        x = x_xT[:, 0:TT * D].rearrange("p (t n) -> p t n", t=TT)
        xT = x_xT[:, TT * D:].rearrange("p (k s) -> p k s", k=KC)
        h = sb("h", [P, TT, D])
        qk = sb("qk", [P, RH, 4, SEQ])
        rv = sb("rv", [P, TT, RH * RV])
        rg = sb("rg", [P, RH, TT, RV])
        aqT = sb("aqT", [P, AH, SEQ])
        stage = sb("stage", [P, 2, TT, NB])
        tmp = sb("tmp", [P, TT, NB])
        sig = sb("sig", [P, TT, NB])
        akT = sb("akT", [P, SEQ])
        av = sb("av", [P, TT, AD])
        mask = sb("mask", [P, P + SEQ])
        wsc = sb("wsc", [P, TT, IH])
        rb = sb("rb", [P, NG + NE])
        m8 = sb("m8", [P, TT, 8])
        i8 = sb("i8", [P, TT, 8], u32)
        stat = sb("stat", [P, TT, 2, 6])
        mv = sb("mv", [P, TT, 2])
        var = sb("var", [P, TT])
        rstd = sb("rstd", [P, TT])
        nwt = sb("nwt", [P, TT])
        nmx = sb("nmx", [P, 4])
        ssum = sb("ssum", [P, 4])
        lg = sb("lg", [P, TT, NG + NE])
        g8 = sb("g8", [P, TT, 8])
        ml = sb("ml", [P, TT, NE])
        e4 = sb("e4", [P, TT, NG])
        gs = sb("gs", [P, TT, 12])
        oh = sb("oh", [P, TT, 2, NE])
        sel = sb("sel", [P, TT, NE])
        gate = sb("gate", [P, TT, NE])
        pos = sb("pos", [P, TT, NE])
        cnt = sb("cnt", [P, 6])
        npass = sb("npass", [P, 1], i32)

        def table(name, lo=0, hi=None):
            return tab[:, TAB[name] + lo:TAB[name] + (TABLES[name] if hi is None else hi)]

        ident = table("ident")
        iota = table("iota")
        causal = table("causal")

        def split(name, home, first, shape):
            return nc.alloc_sbuf_tensor_at(name, shape, f32r,
                                           offset=nc.lookup_mloc(home).addr + 4 * first)

        low = split("w_low", ring, 0, [P, RAW, TILE])
        high = split("w_high", ring, RAW * TILE, [P, HIGH, TILE])
        x_high = split("x_high", x_xT, TT * D, [P, KC, SEQ])
        x_low = split("x_low", ring, (RAW + HIGH) * TILE, [P, KC, SEQ])

        rg_flat = rg[:, :, :, :].rearrange("p a t n -> p (a t n)")
        iqT = rg_flat[:, 0:1024].rearrange("p (b s) -> p b s", s=SEQ)
        ikT = rg_flat[:, 1024:1280]
        score = rg_flat[:, 1280:1280 + P + SEQ]
        prob = rg_flat[:, 1792:3328].rearrange("p (b a s) -> p b a s", b=2, a=2)
        pT = rg_flat[:, 3328:4096].rearrange("p (a s) -> p a s", a=2)
        stage_flat = stage[:, :, :, :].rearrange("p b t n -> p (b t n)")
        dT = stage_flat[:, 0:RH * (P + SEQ)].rearrange("p (a s) -> p a s", a=RH)
        lnp = stage_flat.rearrange("p (c n) -> p c n", c=2)
        retT = qk[:, :, :, :].rearrange("p a c s -> p (a c) s")
        mergedT = aqT
        ga = rv[:, :, 0:D]
        rv_flat = rv[:, :, :].rearrange("p t n -> p (t n)")
        first_pair = [ring[:, 3, :], ring[:, 4, :], ring[:, 5, :], rg_flat, rv_flat, x_xT[:, :]]
        later_pair = [ring[:, s, :] for s in range(RING)]
        qk_flat = qk[:, :, :, :].rearrange("p a c s -> p (a c s)")
        xgT = qk_flat[:, 0:1024].rearrange("p (k s) -> p k s", k=KC)
        msig = qk_flat[:, 1024:1536]
        hid = qk_flat[:, 1536:2048]
        hidT = qk_flat[:, 2048:2560].rearrange("p (j s) -> p j s", j=FC)
        ytok = qk_flat[:, 2560:3584]
        gT = qk_flat[:, 3584:3840]
        aq_flat = aqT[:, :, :].rearrange("p a s -> p (a s)")
        pick = aq_flat[:, 0:256].rearrange("p (t s) -> p t s", t=TT)
        gpick = aq_flat[:, 256:512].rearrange("p (t s) -> p t s", t=TT)
        zeros = aq_flat[:, 512:512 + NB // 2].bitcast(bf16)

        psum = ctx.enter_context(nc.psum_tensor("psum", [P, 8, NB], f32))

        def banks(name):
            g = JOB[name] % GROUPS
            return psum[:, 2 * g:2 * g + 2, :]

        acc = psum[:, 0:4, :].rearrange("p (t n) c -> p t (n c)", t=TT)
        bank_g, bank_u = psum[:, 4, :], psum[:, 5, :]
        bank_y = [psum[:, 6, :], psum[:, 7, :]]
        wide_y = psum[:, 6:8, :].rearrange("p b c -> p (b c)")

        job_free = [sem(f"job_free{g}") for g in range(GROUPS)]
        full_a = [sem(f"full_a{g}") for g in range(GROUPS)]
        full_v = [sem(f"full_v{g}") for g in range(GROUPS)]
        tile_in = [sem(f"tile_in{s}") for s in range(RING)]
        tile_used = sem("tile_used")
        high_ready = sem("high_ready")
        low_ready = sem("low_ready")
        high_used = sem("high_used")
        x_high_ready = sem("x_high_ready")
        outside_in = [sem(f"outside_in{n}") for n in range(OUTSIDE)]
        rg_free, rv_free, x_free = sem("rg_free"), sem("rv_free"), sem("x_free")
        first_in = tile_in[3:6] + outside_in
        start_in = sem("start_in")
        x_ready = sem("x_ready")
        staged = sem("staged")
        dve_step = sem("dve_step")
        act_step = sem("act_step")
        max_ready = sem("max_ready")
        exp_ready = sem("exp_ready")
        p_ready = sem("p_ready")
        sig_ready = sem("sig_ready")
        sig_free = sem("sig_free")
        decayed = sem("decayed")
        yn_ready = sem("yn_ready")
        gates_in = sem("gates_in")
        merged_ready = sem("merged_ready")
        lnp_in = sem("lnp_in")
        rb_in = sem("rb_in")
        h_ready = sem("h_ready")
        router_max = sem("router_max")
        router_exp = sem("router_exp")
        sel_ready = sem("sel_ready")
        npass_pe, npass_act, npass_sp = sem("npass_pe"), sem("npass_act"), sem("npass_sp")
        picked, gpicked = sem("picked"), sem("gpicked")
        xg_full, xg_copied = sem("xg_full"), sem("xg_copied")
        gate_full, silu_in, up_full = sem("gate_full"), sem("silu_in"), sem("up_full")
        hid_ready = sem("hid_ready")
        hidT_full, hidT_copied = sem("hidT_full"), sem("hidT_copied")
        y_full = [sem(f"y_full{n}") for n in range(2)]
        y_copied = [sem(f"y_copied{n}") for n in range(2)]
        tg_full, tg_copied = sem("tg_full"), sem("tg_copied")
        acc_full = sem("acc_full")
        out_in = sem("out_in")

        block = ctx.enter_context(nc.Block())

        win_v = w_in.rearrange("l (p k) n -> l p k n", k=KC)
        ret_v = w_ret_o.rearrange("l (k p) n -> l p k n", p=P)
        dsa_v = w_dsa_o.rearrange("l (k p) n -> l p k n", p=P)
        out_v = w_out.rearrange("l (k p) n -> l p k n", p=P)
        grp_v = grp_w.rearrange("l (p k) n -> l p k n", k=KC)
        exp_v = exp_w.rearrange("l (p k) n -> l p k n", k=KC)
        gate_v = w_gate.rearrange("l e (p k) n -> (l e) p (k n)", k=KC)
        up_v = w_up.rearrange("l e (p k) n -> (l e) p (k n)", k=KC)
        down_v = w_down.rearrange("l e (j p) n -> (l e) p j n", p=P)

        def slot(i, w=NB, of=ring):
            return of[:, i, 0:KC * w].rearrange("p (k n) -> p k n", k=KC)

        def half_tile(of, i, w, b):
            return of[:, i, b * (KC // 2) * w:(b + 1) * (KC // 2) * w]

        @block.sync
        def _(sp):
            def at(v, l):
                return v[bass.ds(l, 1)].rearrange("a p k n -> p (a k) n")

            def load(e, u, tiles, landed, free):
                sp.wait_ge(free, 1).then_inc(free, -1)
                v = (gate_v, up_v, down_v)[u // 2][bass.ds(e + u % 2, 1)]
                if u < 4:
                    sp.dma_start(tiles[u], v.rearrange("a p n -> p (a n)")
                                 ).then_inc(landed[u], 16)
                else:
                    sp.dma_start(tiles[u].rearrange("p (j n) -> p j n", j=FC),
                                 v.rearrange("a p j n -> p (a j) n")).then_inc(landed[u], 16)

            with sp.Fori(0, DEPTH) as l:
                for i, (name, c, w) in enumerate(IN_TILES):
                    if i == RAW:
                        sp.wait_ge(tile_used, RING - RAW).then_inc(tile_used, RAW - RING)
                    sp.wait_ge(tile_used, 1).then_inc(tile_used, -1)
                    sp.dma_start(slot(i % RAW, w), at(win_v, l)[:, :, c:c + w]
                                 ).then_inc(tile_in[i % RAW], 16)
                for i, name in enumerate(TILES):
                    sp.wait_ge(tile_used, 1).then_inc(tile_used, -1)
                    i = i % RING
                    landed = tile_in[i]
                    if name == "router":
                        sp.dma_start(slot(i, NG + NE)[:, :, 0:NG], at(grp_v, l)).then_inc(landed, 16)
                        sp.dma_start(slot(i, NG + NE)[:, :, NG:], at(exp_v, l)).then_inc(landed, 16)
                    else:
                        v = {"dsa": dsa_v, "ret": ret_v, "out": out_v}[name[:3]]
                        n = int(name[3])
                        k = KC * int(name[4]) if name[:3] == "ret" else 0
                        sp.dma_start(slot(i), at(v, l)[:, k:k + KC, n * NB:(n + 1) * NB]
                                     ).then_inc(landed, 16)
                for u, free in enumerate((tile_used, tile_used, tile_used, rg_free, rv_free)):
                    load(l * NE, u, first_pair, first_in, free)
                for u in range(2):
                    load(l * NE + 2, u, later_pair, tile_in, tile_used)
                load(l * NE, 5, first_pair, first_in, x_free)
                for u in range(2, 6):
                    load(l * NE + 2, u, later_pair, tile_in, tile_used)
                sp.wait_ge(npass_sp, 1).then_inc(npass_sp, -1)
                passes = sp.value_load(npass[0:1, 0:1], min_val=1, max_val=SEQ // SLOTS)
                with sp.Fori(2, passes * PAIRS) as q:
                    for u in range(6):
                        load(l * NE + (q % PAIRS) * 2, u, later_pair, tile_in, tile_used)
            sp.wait_ge(x_ready, TT).then_inc(x_ready, -TT)
            sp.dma_start(out.rearrange("o (t p) n -> p (o t) n", p=P), x
                         ).then_inc(out_in, 16)
            sp.wait_ge(out_in, 16)

        @block.tensor
        def _(pe):
            def begin(name):
                g = JOB[name] % GROUPS
                pe.wait_ge(job_free[g], 1).then_inc(job_free[g], -1)
                return psum[:, 2 * g:2 * g + 2, :]

            def finish(name, ins):
                full = full_a if READER[name] == "a" else full_v
                ins.then_inc(full[JOB[name] % GROUPS], 1)

            def copied(name, before):
                if JOB[before] - JOB[name] <= GROUPS:
                    pe.wait_ge(job_free[JOB[name] % GROUPS], 1)

            def product(name, lhs, tiles, w=NB):
                ps = begin(name)
                for n, (tile, lt) in enumerate(zip(tiles, lhs)):
                    i = TILES.index(tile) % RING
                    need = 32 if tile == "router" else 16
                    done = {TILES[0]: 1 + RING - RAW, "router": 0}.get(tile, 1)
                    pe.wait_ge(tile_in[i], need).then_inc(tile_in[i], -need)
                    for t in range(TT):
                        for k in range(KC):
                            mm = nc.tensor.matmul(ps[:, t, 0:w], lt[:, k, t * P:(t + 1) * P],
                                                  slot(i, w)[:, k, :],
                                                  start=(n == 0 and k == 0),
                                                  stop=(n == len(tiles) - 1 and k == KC - 1),
                                                  skip_group_check=len(tiles) > 1)
                            if t == 0 and k == 0 and done:
                                mm.then_inc(tile_used, done)
                finish(name, mm)

            def project(tile):
                i, _, w = IN_TILE[tile]
                ps = begin("P" + tile)
                wh, wl = slot(i % HIGH, w, high), slot(i % RAW, w, low)
                for t in range(TT):
                    for k in range(KC):
                        if t == 0 and k % (KC // 2) == 0:
                            pe.wait_ge(low_ready, 1).then_inc(low_ready, -1)
                        xh, xl = (v[:, k, t * P:(t + 1) * P] for v in (x_high, x_low))
                        for m, (a, b) in enumerate(((xh, wh), (xh, wl), (xl, wh))):
                            mm = nc.tensor.matmul(ps[:, t, 0:w], a, b[:, k, :],
                                                  start=(k == 0 and m == 0),
                                                  stop=(k == KC - 1 and m == 2))
                            if i > 0 and t == 0 and k == 0 and m == 0:
                                mm.then_inc(tile_used, 1)
                            if 0 < i < len(IN_TILES) - 1 and t == 0 and k == 0 and m == 1:
                                mm.then_inc(high_used, 1)
                finish("P" + tile, mm)

            def transposes(name, src, n=4):
                ps = begin(name)
                v = ps.rearrange("p b c -> p (b c)")
                for j in range(n):
                    for t in range(TT):
                        o = v[:, j * SEQ + t * P:j * SEQ + (t + 1) * P]
                        mm = nc.tensor.transpose(o, src(t, j), ident)
                finish(name, mm)

            def turn_rows(names, src, ready, release=0):
                views = [begin(name).rearrange("p b c -> p (b c)") for name in names]
                for t in range(TT):
                    pe.wait_ge(ready, 1).then_inc(ready, -1)
                    for i, name in enumerate(names):
                        for j in range(4):
                            mm = nc.tensor.transpose(
                                views[i][:, j * SEQ + t * P:j * SEQ + (t + 1) * P],
                                src[:, t, 4 * i + j:D:KC], ident)
                            if t == 0 and i == 0 and j == 0 and release:
                                mm.then_inc(tile_used, release)
                        if t == TT - 1:
                            finish(name, mm)

            def turn_stage(tile, b, n=4):
                pe.wait_ge(staged, 1).then_inc(staged, -1)
                transposes("T" + tile, lambda t, j: stage[:, b, t, j * P:(j + 1) * P], n)

            def index_scores(i):
                if i == 0:
                    copied("Tiq", "IX0")
                ps = begin(f"IX{i}")
                for a in range(2):
                    r = slice(a * ID, (a + 1) * ID)
                    for t in range(TT):
                        mm = nc.tensor.matmul(ps[:, a, t * P:P + t * SEQ], iqT[r, i, t * P:(t + 1) * P],
                                              ikT[r, 0:(t + 1) * P], start=True, stop=True)
                finish(f"IX{i}", mm)

            def attention_scores(i):
                ps = begin(f"AS{i}")
                for a in range(2):
                    for t in range(TT):
                        mm = nc.tensor.matmul(ps[:, a, t * P:t * P + (t + 1) * P],
                                              aqT[:, 2 * i + a, t * P:(t + 1) * P],
                                              akT[:, 0:(t + 1) * P], start=True, stop=True)
                finish(f"AS{i}", mm)

            def turn_probs(i):
                pe.wait_ge(p_ready, 1).then_inc(p_ready, -1)
                ps = begin(f"AT{i}")
                for a in range(2):
                    for b in range(3):
                        mm = nc.tensor.transpose(ps[:, a, b * P:(b + 1) * P],
                                                 prob[:, i % 2, a, b * P:(b + 1) * P], ident)
                finish(f"AT{i}", mm)

            def attend(i):
                copied(f"AT{i}", f"AO{i}")
                ps = begin(f"AO{i}").rearrange("p b c -> p (b c)")
                for a in range(2):
                    o = ps[:, a * SEQ:(a + 1) * SEQ]
                    nc.tensor.matmul(o[:, 0:P], av[:, 0, :], pT[:, a, 0:P], start=True, stop=True)
                    nc.tensor.matmul(o[:, P:SEQ], av[:, 0, :], pT[:, a, P:SEQ],
                                     start=True, stop=False)
                    mm = nc.tensor.matmul(o[:, P:SEQ], av[:, 1, :], pT[:, a, SEQ:SEQ + P],
                                          start=False, stop=True)
                finish(f"AO{i}", mm)

            def retention_scores(i):
                ps = begin(f"RS{i}")
                for a in range(2):
                    q = qk[:, 2 * i + a, 0:2, :]
                    k = qk[:, 2 * i + a, 2:4, :]
                    for m, (lo, hi) in enumerate(((0, SEQ), (SEQ, SEQ + P))):
                        for c in range(2):
                            mm = nc.tensor.matmul(ps[:, a, lo:hi], k[:, c, m * P:(m + 1) * P],
                                                  q[:, c, m * P:SEQ], start=(c == 0), stop=(c == 1))
                finish(f"RS{i}", mm)

            def retention_values(i):
                if i % 2 == 0:
                    pe.wait_ge(decayed, 1).then_inc(decayed, -1)
                ps = begin(f"RY{i}")
                v = rv[:, :, i * RV:(i + 1) * RV]
                nc.tensor.matmul(ps[:, 0, :], dT[:, i, 0:P], v[:, 0, :], start=True, stop=True)
                nc.tensor.matmul(ps[:, 1, :], dT[:, i, P:SEQ], v[:, 0, :], start=True, stop=False)
                mm = nc.tensor.matmul(ps[:, 1, :], dT[:, i, SEQ:SEQ + P], v[:, 1, :],
                                      start=False, stop=True)
                finish(f"RY{i}", mm)

            def turn_retention(i):
                pe.wait_ge(yn_ready, 1).then_inc(yn_ready, -1)
                transposes(f"RT{i}", lambda t, j: rg[:, i, t, j * P:(j + 1) * P])

            def gather():
                pe.wait_ge(picked, 1).then_inc(picked, -1)
                for k in range(KC):
                    for t in range(TT):
                        mm = nc.tensor.matmul(wide_y[:, k * P:(k + 1) * P], h[:, t, k:D:KC],
                                              pick[:, t, :], start=(t == 0), stop=(t == TT - 1))
                mm.then_inc(xg_full, 1)

            def pair_product(bank, lhs, chunks, tiles, lo, release):
                for k in range(chunks):
                    for e in range(2):
                        w = tiles[e].rearrange("p (k n) -> p k n", k=chunks)
                        mm = nc.tensor.matmul(bank[e * SLOTS:(e + 1) * SLOTS, :],
                                              lhs[:, k, e * SLOTS:(e + 1) * SLOTS],
                                              w[:, k, lo:lo + NB], start=(k == 0),
                                              stop=(k == chunks - 1))
                        if k == 0 and e == 0 and release:
                            mm.then_inc(tile_used, release)
                return mm

            def arrived(sems):
                for landed in sems:
                    pe.wait_ge(landed, 16).then_inc(landed, -16)

            def combine(release=0):
                for t in range(TT):
                    for n in range(2):
                        mm = nc.tensor.matmul(acc[:, t, n * NB:(n + 1) * NB],
                                              gT[:, t * P:(t + 1) * P],
                                              ytok[:, n * NB:(n + 1) * NB], start=False,
                                              stop=False, skip_group_check=True)
                        if t == 0 and n == 0 and release:
                            mm.then_inc(tile_used, release)

            def outputs_copied():
                for n in range(2):
                    pe.wait_ge(y_copied[n], 1).then_inc(y_copied[n], -1)

            def experts(first=False, tiles=later_pair, landed=tile_in, done=(2, 2, 2)):
                if first:
                    pe.wait_ge(xg_copied, 1).then_inc(xg_copied, -1)
                arrived(landed[0:2])
                pair_product(bank_g, xgT, KC, tiles[0:2], 0, done[0]).then_inc(gate_full, 1)
                if not first:
                    pe.wait_ge(tg_copied, 1).then_inc(tg_copied, -1)
                arrived(landed[2:4])
                pair_product(bank_u, xgT, KC, tiles[2:4], 0, done[1]).then_inc(up_full, 1)
                if not first:
                    outputs_copied()
                gather()
                pe.wait_ge(hid_ready, 1).then_inc(hid_ready, -1)
                for j in range(FC):
                    mm = nc.tensor.transpose(bank_g[:, j * P:(j + 1) * P],
                                             hid[:, j * P:(j + 1) * P], ident)
                mm.then_inc(hidT_full, 1)
                if not first:
                    combine()
                pe.wait_ge(gpicked, 1).then_inc(gpicked, -1)
                for t in range(TT):
                    mm = nc.tensor.transpose(bank_u[:, t * P:(t + 1) * P], gpick[:, t, :], ident)
                mm.then_inc(tg_full, 1)
                pe.wait_ge(hidT_copied, 1).then_inc(hidT_copied, -1)
                pe.wait_ge(xg_copied, 1).then_inc(xg_copied, -1)
                arrived(landed[4:6])
                for n in range(2):
                    pair_product(bank_y[n], hidT, FC, tiles[4:6], n * NB, done[2] * (n == 0)
                                 ).then_inc(y_full[n], 1)

            def sum_up_last():
                outputs_copied()
                pe.wait_ge(tg_copied, 1).then_inc(tg_copied, -1)
                combine(1)

            with pe.Fori(0, DEPTH) as l:
                turn_rows(("XT0", "XT1"), x, x_ready)
                copied("XT0", "Pikw")
                copied("XT1", "Pikw")
                project("ikw")
                project("iq")
                turn_stage("ikw", 0, 1)
                project("ak")
                turn_stage("iq", 1)
                project("aq0")
                turn_stage("ak", 0, 1)
                index_scores(0)
                index_scores(1)
                project("aq1")
                turn_stage("aq0", 1)
                index_scores(2)
                index_scores(3)
                project("rq0")
                turn_stage("aq1", 0)
                project("rq1")
                turn_stage("rq0", 1)
                project("rk0")
                turn_stage("rq1", 0)
                project("rk1")
                turn_stage("rk0", 1)
                project("rv0")
                turn_stage("rk1", 0)
                attention_scores(0)
                project("rv1")
                turn_probs(0)
                attention_scores(1)
                project("rv2")
                attend(0)
                turn_probs(1)
                attention_scores(2)
                project("rv3")
                attend(1)
                turn_probs(2)
                attention_scores(3)
                project("rg0")
                attend(2)
                turn_probs(3)
                retention_scores(0)
                retention_scores(1)
                project("rg1")
                attend(3)
                project("rg2")
                retention_values(0)
                project("rg3")
                retention_values(1)
                project("gr0")
                turn_retention(0)
                retention_values(2)
                project("gr1")
                turn_retention(1)
                retention_values(3)
                project("ga0")
                turn_retention(2)
                project("ga1")
                turn_retention(3)
                product("DO0", [aqT], ["dsa0"])
                product("DO1", [aqT], ["dsa1"])
                copied("RT3", "RO0")
                for n in range(2):
                    product(f"RO{n}", [retT[:, 0:KC, :], retT[:, KC:, :]], [f"ret{n}0", f"ret{n}1"])
                for i in range(2):
                    pe.wait_ge(merged_ready, 1).then_inc(merged_ready, -1)
                    transposes(f"MT{i}", lambda t, j: h[:, t, (4 * i + j) * P:(4 * i + j + 1) * P])
                copied("MT0", "OUT0")
                copied("MT1", "OUT0")
                for n in range(2):
                    product(f"OUT{n}", [mergedT], [f"out{n}"])
                turn_rows(("HT0", "HT1"), h, h_ready, 1)
                copied("HT0", "RL")
                copied("HT1", "RL")
                product("RL", [xT], ["router"], NG + NE)
                pe.wait_ge(sel_ready, 1).then_inc(sel_ready, -1)
                ps = begin("PC")
                nc.tensor.matmul(ps[:, 0, 0:NE], table("before"), sel[:, 0, :], start=True, stop=True
                                 ).then_inc(tile_used, 1)
                for c, m in ((1, "before"), (2, "ones")):
                    nc.tensor.matmul(ps[:, 0, c * NE:(c + 1) * NE], table("ones"), sel[:, 0, :],
                                     start=True, stop=False)
                    mm = nc.tensor.matmul(ps[:, 0, c * NE:(c + 1) * NE], table(m), sel[:, 1, :],
                                          start=False, stop=True)
                finish("PC", mm)
                for g in range(GROUPS):
                    pe.wait_ge(job_free[g], 1)
                pe.wait_ge(npass_pe, 1).then_inc(npass_pe, -1)
                for b in range(4):
                    nc.tensor.matmul(psum[:, b, :], zeros[:, 0:P], zeros, start=True,
                                     stop=False, skip_group_check=True)
                passes = pe.value_load(npass[0:1, 0:1], min_val=1, max_val=SEQ // SLOTS)
                gather()
                experts(first=True, tiles=first_pair, landed=first_in, done=(0, 2, 1))
                experts(done=(0, 2, 2))
                with pe.Fori(2, passes * PAIRS) as _q:
                    experts()
                sum_up_last()
                for b in range(4):
                    mm = nc.tensor.matmul(psum[:, b, :], zeros[:, 0:P], zeros, start=False,
                                          stop=True, skip_group_check=True)
                    if b == 0:
                        mm.then_inc(tile_used, 1)
                mm.then_inc(acc_full, 1)

        @block.scalar
        def _(act):
            def take(name):
                g = JOB[name] % GROUPS
                act.wait_ge(full_a[g], 1).then_inc(full_a[g], -1)
                return psum[:, 2 * g:2 * g + 2, :]

            def copy_out(name, dst, n=1024):
                src = take(name).rearrange("p b c -> p (b c)")[:, 0:n]
                if len(dst.shape) == 3:
                    src = src.rearrange("p (a b) -> p a b", a=dst.shape[1])
                elif len(dst.shape) == 4:
                    src = src.rearrange("p (a b c) -> p a b c", a=dst.shape[1], b=dst.shape[2])
                nc.scalar.activation(dst, src, ACT.Copy).then_inc(job_free[JOB[name] % GROUPS], 1)

            def split_x(i):
                src = take(f"XT{i}").rearrange("p b (a s) -> p (b a) s", s=SEQ)
                nc.scalar.activation(x_high[:, 4 * i:4 * i + 4, :], src, ACT.Copy
                                     ).then_inc(x_high_ready, 1)

            def split_high(i):
                w = IN_TILES[i][2]
                act.wait_ge(tile_in[i % RAW], 16).then_inc(tile_in[i % RAW], -16)
                if i >= HIGH:
                    act.wait_ge(high_used, 1).then_inc(high_used, -1)
                for b in range(2):
                    nc.scalar.activation(half_tile(high, i % HIGH, w, b),
                                         half_tile(ring, i % RAW, w, b), ACT.Copy
                                         ).then_inc(high_ready, 1)

            def exps(i):
                act.wait_ge(max_ready, 1).then_inc(max_ready, -1)
                for a in range(2):
                    for t in range(TT):
                        v = prob[:, i % 2, a, t * P:P + t * SEQ]
                        e = nc.scalar.activation(v, v, ACT.Exp, bias=nmx[:, 2 * t + a:2 * t + a + 1],
                                                 accum_out=ssum[:, 2 * t + a:2 * t + a + 1])
                        if (a, t) != (1, TT - 1):
                            e.then_inc(act_step, 1)
                            act.wait_ge(act_step, 1).then_inc(act_step, -1)
                e.then_inc(exp_ready, 1)

            def silu_gate(n):
                ps = take(f"Prg{n}")
                act.wait_ge(sig_free, 1).then_inc(sig_free, -1)
                nc.scalar.activation(sig[:, :, :], ps, ACT.Sigmoid).then_inc(sig_ready, 1)

            def branch_gate(name, dst):
                ps = take("P" + name)
                g = JOB["P" + name] % GROUPS
                nc.scalar.activation(dst, ps, ACT.Sigmoid).then_inc(act_step, 1)
                act.wait_ge(act_step, 1).then_inc(act_step, -1)
                act.sem_inc(job_free[g], 1)
                act.sem_inc(gates_in, 1)

            def experts():
                act.wait_ge(gate_full, 1).then_inc(gate_full, -1)
                nc.scalar.activation(msig, bank_g, ACT.Sigmoid).then_inc(silu_in, 1)
                act.wait_ge(hidT_full, 1).then_inc(hidT_full, -1)
                nc.scalar.activation(hidT, bank_g.rearrange("p (j s) -> p j s", j=FC), ACT.Copy
                                     ).then_inc(hidT_copied, 1)
                act.wait_ge(tg_full, 1).then_inc(tg_full, -1)
                nc.scalar.activation(gT, bank_u[:, 0:SEQ], ACT.Copy).then_inc(tg_copied, 1)
                for n in range(2):
                    act.wait_ge(y_full[n], 1).then_inc(y_full[n], -1)
                    nc.scalar.activation(ytok[:, n * NB:(n + 1) * NB], bank_y[n], ACT.Copy
                                         ).then_inc(y_copied[n], 1)

            def ln_params(g, b, l):
                for n, v in enumerate((g, b)):
                    act.dma_start(lnp[:, n, :], v[bass.ds(l, 1)].broadcast_to((P, D))
                                  ).then_inc(lnp_in, 16)

            act.dma_start(x, x_in.rearrange("o (t p) n -> p (o t) n", p=P)
                          ).then_inc(start_in, 16)
            act.dma_start(tab[:, :], tables).then_inc(start_in, 16)
            with act.Fori(0, DEPTH) as l:
                act.dma_start(rb[:, 0:NG], grp_b[bass.ds(l, 1)].broadcast_to((P, NG))
                              ).then_inc(rb_in, 16)
                act.dma_start(rb[:, NG:], exp_b[bass.ds(l, 1)].broadcast_to((P, NE))
                              ).then_inc(rb_in, 16)
                split_high(0)
                split_x(0)
                split_x(1)
                split_high(1)
                split_high(2)
                copy_out("Tikw", ikT, SEQ)
                split_high(3)
                copy_out("Tiq", iqT)
                split_high(4)
                copy_out("Tak", akT[:, :], SEQ)
                split_high(5)
                copy_out("Taq0", aqT[:, 0:4, :])
                split_high(6)
                copy_out("Taq1", aqT[:, 4:8, :])
                split_high(7)
                copy_out("Trq0", qk[:, 0:2, 0:2, :])
                split_high(8)
                copy_out("Trq1", qk[:, 2:4, 0:2, :])
                split_high(9)
                copy_out("Trk0", qk[:, 0:2, 2:4, :])
                split_high(10)
                copy_out("Prv0", rv[:, :, 0:NB])
                copy_out("Trk1", qk[:, 2:4, 2:4, :])
                for i in range(4):
                    split_high(11 + i)
                    exps(i)
                    if i < 3:
                        copy_out(f"Prv{i + 1}", rv[:, :, (i + 1) * NB:(i + 2) * NB])
                    else:
                        silu_gate(0)
                    if i >= 1:
                        copy_out(f"AO{i - 1}", aqT[:, 2 * i - 2:2 * i, :], 2 * SEQ)
                    turned = take(f"AT{i}")
                    nc.scalar.activation(pT[:, :, :], turned[:, :, 0:P + SEQ], ACT.Copy
                                         ).then_inc(job_free[JOB[f"AT{i}"] % GROUPS], 1)
                split_high(15)
                silu_gate(1)
                copy_out("AO3", aqT[:, 6:8, :], 2 * SEQ)
                split_high(16)
                silu_gate(2)
                split_high(17)
                silu_gate(3)
                split_high(18)
                branch_gate("gr0", h[:, :, 0:NB])
                copy_out("RT0", retT[:, 0:4, :])
                split_high(19)
                branch_gate("gr1", h[:, :, NB:D])
                copy_out("RT1", retT[:, 4:8, :])
                split_high(20)
                branch_gate("ga0", ga[:, :, 0:NB])
                copy_out("RT2", retT[:, 8:12, :])
                branch_gate("ga1", ga[:, :, NB:D])
                copy_out("RT3", retT[:, 12:16, :])
                act.sem_inc(rg_free, 1)
                ln_params(ln1_g, ln1_b, l)
                for i in range(2):
                    copy_out(f"MT{i}", mergedT[:, 4 * i:4 * i + 4, :])
                for i in range(2):
                    copy_out(f"HT{i}", xT[:, 4 * i:4 * i + 4, :])
                act.wait_ge(router_max, 1).then_inc(router_max, -1)
                ln_params(ln2_g, ln2_b, l)
                for t in range(TT):
                    nc.scalar.activation(e4[:, t, :], lg[:, t, 0:NG], ACT.Exp,
                                         bias=gs[:, t, 0:1], accum_out=gs[:, t, 1:2]
                                         ).then_inc(act_step, 1)
                    act.wait_ge(act_step, 1).then_inc(act_step, -1)
                nc.scalar.activation(gs[:, :, 3:4], gs[:, :, 2:3], ACT.Exp).then_inc(router_exp, 1)
                act.wait_ge(npass_act, 1).then_inc(npass_act, -1)
                passes = act.value_load(npass[0:1, 0:1], min_val=1, max_val=SEQ // SLOTS)
                with act.Fori(0, passes * PAIRS) as _q:
                    experts()

        @block.vector
        def _(dve):
            V = nc.vector

            def step(ins):
                ins.then_inc(dve_step, 1)
                dve.wait_ge(dve_step, 1).then_inc(dve_step, -1)

            def take(name):
                g = JOB[name] % GROUPS
                dve.wait_ge(full_v[g], 1).then_inc(full_v[g], -1)
                return psum[:, 2 * g:2 * g + 2, :]

            def free(name):
                dve.sem_inc(job_free[JOB[name] % GROUPS], 1)

            def rotate(name, b, half, heads):
                ps = take(name)
                w = 2 * half * heads
                for t in range(TT):
                    src = ps[:, t, 0:w].rearrange("p (a d) -> p a d", d=half)
                    for fn, dst in (("cos", tmp), ("sin", sig)):
                        f = table(fn, t * P, (t + 1) * P)[:, 0:P:P // half]
                        last = V.tensor_tensor(
                            dst[:, t, 0:w].rearrange("p (a d) -> p a d", d=half), src,
                            f.unsqueeze(1).broadcast_to((P, 2 * heads, half)), ALU.mult)
                step(last)
                for t in range(TT):
                    def halves(a):
                        v = a.rearrange("p (a c d) -> p a c d", c=2, d=half)
                        return v[:, :, 0, :], v[:, :, 1, :]
                    (c1, c2), (s1, s2) = halves(tmp[:, t, 0:w]), halves(sig[:, t, 0:w])
                    o1, o2 = halves(stage[:, b, t, 0:w])
                    V.tensor_tensor(o1, c1, s2, ALU.subtract)
                    last = V.tensor_tensor(o2, c2, s1, ALU.add)
                step(last)
                return ps

            def norm_stats(n):
                for t in range(TT):
                    last = V.bn_aggr(mv[:, t, :], stat[:, t, 0:n, :].rearrange("p a b -> p (a b)"))
                step(last)
                step(V.tensor_scalar(var[:, :], mv[:, :, 1], EPS, None, ALU.add))
                step(V.tensor_scalar(rstd[:, :].bitcast(i32), var[:, :].bitcast(i32), 1, None,
                                     ALU.logical_shift_right))
                step(V.tensor_scalar(rstd[:, :].bitcast(i32), rstd[:, :].bitcast(i32), -1.0,
                                     float(0x5F3759DF), ALU.mult, ALU.add))
                for _ in range(3):
                    step(V.tensor_tensor(nwt[:, :], rstd[:, :], rstd[:, :], ALU.mult))
                    step(V.scalar_tensor_tensor(out=nwt[:, :], in0=nwt[:, :], scalar=-0.5,
                                                in1=var[:, :], op0=ALU.mult, op1=ALU.mult))
                    step(V.scalar_tensor_tensor(out=rstd[:, :], in0=nwt[:, :], scalar=1.5,
                                                in1=rstd[:, :], op0=ALU.add, op1=ALU.mult))

            def halves_stats(src, n):
                for t in range(TT):
                    last = V.bn_stats(stat[:, t, n, :], src[:, t, n * NB:(n + 1) * NB])
                step(last)

            def layer_norm(src, dst, done):
                norm_stats(2)
                step(V.tensor_scalar(mv[:, :, 0], mv[:, :, 0], -1.0, None, ALU.mult))
                dve.wait_ge(lnp_in, 32).then_inc(lnp_in, -32)
                for t in range(TT):
                    step(V.scalar_tensor_tensor(out=dst[:, t, :], in0=src[:, t, :],
                                                scalar=mv[:, t, 0:1], in1=lnp[:, 0, :],
                                                op0=ALU.add, op1=ALU.mult))
                    V.scalar_tensor_tensor(out=dst[:, t, :], in0=dst[:, t, :],
                                           scalar=rstd[:, t:t + 1], in1=lnp[:, 1, :],
                                           op0=ALU.mult, op1=ALU.add).then_inc(done, 1)

            def index_scores(i):
                ps = take(f"IX{i}")
                for a in range(2):
                    hd = 2 * i + a
                    for t in range(TT):
                        lo, hi = t * P, P + t * SEQ
                        last = V.tensor_scalar(tmp[:, 0, lo:hi], ps[:, a, lo:hi], 0.0,
                                               wsc[:, t, hd:hd + 1], ALU.max, ALU.mult)
                    step(last)
                    if a == 1:
                        free(f"IX{i}")
                    prev = causal if hd == 0 else score
                    step(V.tensor_tensor(score, prev, tmp[:, 0, 0:P + SEQ], ALU.add))

            def select(last_half):
                for _ in range(TOPK // 16):
                    for t in range(TT):
                        last = V.max(m8[:, t, :], score[:, t * P:P + t * SEQ])
                    step(last)
                    for t in range(TT):
                        v = score[:, t * P:P + t * SEQ]
                        last = V.match_replace(v, m8[:, t, :], v, TAKEN)
                    step(last)
                if not last_half:
                    return
                step(V.tensor_scalar(score, score, TAKEN, 1.0, ALU.is_equal, ALU.subtract))
                step(V.scalar_tensor_tensor(out=mask[:, :], in0=score, scalar=BIG, in1=causal,
                                            op0=ALU.mult, op1=ALU.min))

            def split_x(i):
                dve.wait_ge(x_high_ready, 1).then_inc(x_high_ready, -1)
                src = banks(f"XT{i}").rearrange("p b (a s) -> p (b a) s", s=SEQ)
                c = slice(4 * i, 4 * i + 4)
                V.tensor_tensor(x_low[:, c, :], src, x_high[:, c, :].bitcast(f32), ALU.subtract
                                ).then_inc(job_free[JOB[f"XT{i}"] % GROUPS], 1)

            def split_low(i):
                w = IN_TILES[i][2]
                for b in range(2):
                    dve.wait_ge(high_ready, 1).then_inc(high_ready, -1)
                    V.tensor_tensor(half_tile(low, i % RAW, w, b), half_tile(ring, i % RAW, w, b),
                                    half_tile(high, i % HIGH, w, b).bitcast(f32), ALU.subtract
                                    ).then_inc(low_ready, 1)

            def softmax(i, tile):
                ps = take(f"AS{i}")
                pr = prob[:, i % 2, :, :]
                for a in range(2):
                    last = V.scalar_tensor_tensor(out=pr[:, a, :], in0=ps[:, a, 0:P + SEQ],
                                                  scalar=AD ** -0.5, in1=mask[:, :],
                                                  op0=ALU.mult, op1=ALU.add)
                step(last)
                free(f"AS{i}")
                for t in range(TT):
                    last = V.tensor_reduce(nmx[:, 2 * t:2 * t + 2], pr[:, :, t * P:P + t * SEQ], X,
                                           ALU.max)
                step(last)
                step(V.tensor_scalar(nmx[:, :], nmx[:, :], -1.0, None, ALU.mult))
                dve.sem_inc(max_ready, 1)
                split_low(tile)
                dve.wait_ge(exp_ready, 1).then_inc(exp_ready, -1)
                step(V.reciprocal(ssum[:, :], ssum[:, :]))
                for a in range(2):
                    for t in range(TT):
                        v = pr[:, a, t * P:P + t * SEQ]
                        last = V.tensor_scalar(v, v, ssum[:, 2 * t + a:2 * t + a + 1], None,
                                               ALU.mult)
                last.then_inc(p_ready, 1)

            def silu(n):
                dve.wait_ge(sig_ready, 1).then_inc(sig_ready, -1)
                step(V.tensor_tensor(rg[:, n, :, :], banks(f"Prg{n}"), sig[:, :, :], ALU.mult))
                free(f"Prg{n}")
                dve.sem_inc(sig_free, 1)

            def decay(i):
                ps = take(f"RS{i}")
                for a in range(2):
                    hd = 2 * i + a
                    d = table("decay", hd * SEQ, (hd + 1) * SEQ)
                    V.tensor_tensor(dT[:, hd, 0:SEQ], ps[:, a, 0:SEQ], d, ALU.mult)
                    last = V.tensor_tensor(dT[:, hd, SEQ:SEQ + P], ps[:, a, SEQ:SEQ + P],
                                           d[:, 0:P], ALU.mult)
                step(last)
                free(f"RS{i}")
                dve.sem_inc(decayed, 1)

            def group_norm(i):
                ps = take(f"RY{i}")
                for t in range(TT):
                    last = V.bn_stats(stat[:, t, 0, :], ps[:, t, :])
                step(last)
                norm_stats(1)
                for t in range(TT):
                    last = V.tensor_scalar(tmp[:, t, :], ps[:, t, :], mv[:, t, 0:1],
                                           rstd[:, t:t + 1], ALU.subtract, ALU.mult)
                step(last)
                free(f"RY{i}")
                step(V.tensor_tensor(rg[:, i, :, :], rg[:, i, :, :], tmp[:, :, :], ALU.mult))
                dve.sem_inc(yn_ready, 1)

            def best(v):
                for t in range(TT):
                    last = V.max(m8[:, t, :], v[:, t, :])
                step(last)
                for t in range(TT):
                    last = V.max_index(i8[:, t, :], m8[:, t, :], v[:, t, :])
                step(last)

            def router():
                ps = take("RL")
                dve.sem_inc(x_free, 1)
                V.memset(zeros, 0.0)
                dve.wait_ge(rb_in, 32).then_inc(rb_in, -32)
                for t in range(TT):
                    step(V.tensor_tensor(lg[:, t, :], ps[:, t, 0:NG + NE], rb[:, :], ALU.add))
                free("RL")
                step(V.tensor_copy(g8[:, :, 0:NG], lg[:, :, 0:NG]))
                best(g8)
                V.tensor_scalar(gs[:, :, 0:1], m8[:, :, 0:1], -1.0, None, ALU.mult)
                step(V.tensor_copy(gs[:, :, 4:5], i8[:, :, 0:1]))
                step(V.tensor_tensor(oh[:, :, 0, 0:NG],
                                     iota[:, 0:NG].unsqueeze(1).broadcast_to((P, TT, NG)),
                                     gs[:, :, 4:5].broadcast_to((P, TT, NG)), ALU.is_equal))
                step(V.tensor_scalar(oh[:, :, 0, 0:NG], oh[:, :, 0, 0:NG], 1.0, BIG,
                                     ALU.subtract, ALU.mult))
                for t in range(TT):
                    last = V.tensor_tensor(
                        ml[:, t, :].rearrange("p (g e) -> p g e", g=NG),
                        lg[:, t, NG:].rearrange("p (g e) -> p g e", g=NG),
                        oh[:, t, 0, 0:NG].unsqueeze(2).broadcast_to((P, NG, EPG)), ALU.add)
                step(last)
                best(ml)
                V.tensor_tensor(gs[:, :, 2:3], m8[:, :, 1:2], m8[:, :, 0:1], ALU.subtract)
                step(V.tensor_copy(gs[:, :, 5:7], i8[:, :, 0:2]))
                for c in range(2):
                    for t in range(TT):
                        last = V.tensor_scalar(oh[:, t, c, :], iota[:, 0:NE], gs[:, t, 5 + c:6 + c],
                                               None, ALU.is_equal)
                step(last)
                step(V.tensor_tensor(sel[:, :, :], oh[:, :, 0, :], oh[:, :, 1, :], ALU.add))
                dve.sem_inc(router_max, 1)
                dve.sem_inc(sel_ready, 1)

            def gates():
                dve.wait_ge(router_exp, 1).then_inc(router_exp, -1)
                step(V.tensor_scalar(gs[:, :, 7:8], gs[:, :, 3:4], 1.0, None, ALU.add))
                step(V.tensor_tensor(gs[:, :, 7:8], gs[:, :, 7:8], gs[:, :, 1:2], ALU.mult))
                step(V.reciprocal(gs[:, :, 7:8], gs[:, :, 7:8]))
                step(V.tensor_tensor(gs[:, :, 8:9], gs[:, :, 7:8], gs[:, :, 3:4], ALU.mult))
                for t in range(TT):
                    step(V.tensor_scalar(gate[:, t, :], oh[:, t, 0, :], gs[:, t, 7:8], None,
                                         ALU.mult))
                    step(V.scalar_tensor_tensor(out=gate[:, t, :], in0=oh[:, t, 1, :],
                                                scalar=gs[:, t, 8:9], in1=gate[:, t, :],
                                                op0=ALU.mult, op1=ALU.add))

            def places():
                ps = take("PC")
                pc = ps[:, 0, 0:3 * NE].rearrange("p (c e) -> p c e", c=3)
                for t in range(TT):
                    step(V.scalar_tensor_tensor(out=pos[:, t, :], in0=pc[:, t, :], scalar=1.0,
                                                in1=sel[:, t, :], op0=ALU.add, op1=ALU.mult))
                step(V.tensor_scalar(pos[:, :, :], pos[:, :, :], -1.0, None, ALU.add))
                step(V.tensor_reduce(cnt[:, 0:1], pc[:, 2, :], X, ALU.max))
                free("PC")
                step(V.tensor_scalar(cnt[:, 1:5], table("passes"), cnt[:, 0:1], None, ALU.is_lt))
                step(V.tensor_reduce(cnt[:, 5:6], cnt[:, 1:5], X, ALU.add))
                step(V.tensor_copy(npass[:, :], cnt[:, 5:6]))
                dve.sem_inc(npass_sp, 1)
                dve.sem_inc(npass_pe, 1)
                dve.sem_inc(npass_act, 1)

            def lists(e0):
                for e in range(2):
                    for t in range(TT):
                        last = V.tensor_scalar(pick[:, t, e * SLOTS:(e + 1) * SLOTS], iota,
                                               pos[:, t, bass.ds(e0 + e, 1)], None, ALU.is_equal)
                last.then_inc(picked, 1)

            def gathered():
                dve.wait_ge(xg_full, 1).then_inc(xg_full, -1)
                V.tensor_copy(xgT, wide_y.rearrange("p (k s) -> p k s", k=KC)
                              ).then_inc(xg_copied, 1)

            def experts(e0, ends_pass):
                dve.wait_ge(silu_in, 1).then_inc(silu_in, -1)
                step(V.tensor_tensor(msig, bank_g, msig, ALU.mult))
                for e in range(2):
                    for t in range(TT):
                        c = slice(e * SLOTS, (e + 1) * SLOTS)
                        last = V.tensor_scalar(gpick[:, t, c], pick[:, t, c],
                                               gate[:, t, bass.ds(e0 + e, 1)], None, ALU.mult)
                step(last)
                dve.sem_inc(gpicked, 1)
                if ends_pass:
                    step(V.tensor_scalar(pos[:, :, :], pos[:, :, :], -float(SLOTS), None, ALU.add))
                lists(0 if ends_pass else e0 + 2)
                dve.wait_ge(up_full, 1).then_inc(up_full, -1)
                V.tensor_tensor(hid, msig, bank_u, ALU.mult).then_inc(hid_ready, 1)
                gathered()

            step(V.memset(g8[:, :, :], -BIG))
            for g in range(GROUPS):
                dve.sem_inc(job_free[g], 1)
            dve.sem_inc(tile_used, RING)
            dve.sem_inc(sig_free, 1)
            dve.wait_ge(start_in, 32)
            dve.sem_inc(x_ready, TT)
            with dve.Fori(0, DEPTH) as l:
                split_low(0)
                split_x(0)
                split_x(1)
                split_low(1)
                ps = rotate("Pikw", 0, ID // 2, 1)
                for t in range(TT):
                    step(V.tensor_copy(stage[:, 0, t, ID:2 * ID], stage[:, 0, t, 0:ID]))
                step(V.tensor_scalar(wsc[:, :, :], ps[:, :, ID:ID + IH], IDX_SCALE, None, ALU.mult))
                free("Pikw")
                dve.sem_inc(staged, 1)
                split_low(2)
                rotate("Piq", 1, ID // 2, IH)
                free("Piq")
                dve.sem_inc(staged, 1)
                split_low(3)
                ps = rotate("Pak", 0, AD // 2, 1)
                step(V.tensor_copy(av[:, :, :], ps[:, :, AD:2 * AD]))
                free("Pak")
                dve.sem_inc(staged, 1)
                split_low(4)
                rotate("Paq0", 1, AD // 2, 4)
                free("Paq0")
                dve.sem_inc(staged, 1)
                index_scores(0)
                split_low(5)
                index_scores(1)
                rotate("Paq1", 0, AD // 2, 4)
                free("Paq1")
                dve.sem_inc(staged, 1)
                index_scores(2)
                split_low(6)
                index_scores(3)
                for n, name in enumerate(("rq0", "rq1", "rk0", "rk1")):
                    rotate("P" + name, (n + 1) % 2, RQK // 2, 2)
                    free("P" + name)
                    dve.sem_inc(staged, 1)
                    split_low(7 + n)
                    if n in (1, 2):
                        select(n == 2)
                for i in range(4):
                    softmax(i, 11 + i)
                silu(0)
                decay(0)
                decay(1)
                split_low(15)
                silu(1)
                split_low(16)
                silu(2)
                group_norm(0)
                split_low(17)
                silu(3)
                for i in range(1, RH):
                    split_low(17 + i)
                    group_norm(i)
                dve.wait_ge(gates_in, 4).then_inc(gates_in, -4)
                for n in range(2):
                    ps = take(f"DO{n}")
                    c = slice(n * NB, (n + 1) * NB)
                    step(V.tensor_tensor(ga[:, :, c], ga[:, :, c], ps, ALU.mult))
                    free(f"DO{n}")
                for n in range(2):
                    ps = take(f"RO{n}")
                    c = slice(n * NB, (n + 1) * NB)
                    step(V.tensor_tensor(h[:, :, c], h[:, :, c], ps, ALU.mult))
                    free(f"RO{n}")
                    step(V.tensor_tensor(h[:, :, c], h[:, :, c], ga[:, :, c], ALU.add))
                    dve.sem_inc(merged_ready, 1)
                dve.sem_inc(rv_free, 1)
                for n in range(2):
                    ps = take(f"OUT{n}")
                    c = slice(n * NB, (n + 1) * NB)
                    step(V.scalar_tensor_tensor(out=x[:, :, c], in0=x[:, :, c], scalar=ALPHA,
                                                in1=ps, op0=ALU.mult, op1=ALU.add))
                    free(f"OUT{n}")
                    halves_stats(x, n)
                layer_norm(x, h, h_ready)
                router()
                places()
                passes = dve.value_load(npass[0:1, 0:1], min_val=1, max_val=SEQ // SLOTS)
                lists(0)
                gates()
                gathered()
                with dve.Fori(0, passes) as _p:
                    with dve.Fori(0, PAIRS - 1) as j:
                        experts(j * 2, False)
                    experts(NE - 2, True)
                dve.wait_ge(acc_full, 1).then_inc(acc_full, -1)
                for t in range(TT):
                    last = V.scalar_tensor_tensor(out=x[:, t, :], in0=h[:, t, :], scalar=ALPHA,
                                                  in1=acc[:, t, :], op0=ALU.mult, op1=ALU.add)
                step(last)
                for n in range(2):
                    halves_stats(x, n)
                layer_norm(x, x, x_ready)


_INS = ['x', 'w_in', 'w_ret_o', 'w_dsa_o', 'w_out', 'ln1_g', 'ln1_b', 'router_grp_w',
        'router_grp_b', 'router_exp_w', 'router_exp_b', 'w_gate', 'w_up', 'w_down', 'ln2_g',
        'ln2_b']


def kernel(**inputs):
    import concourse.bacc as _bacc
    from concourse.bass_utils import run_bass_kernel_spmd as _run

    nc = _bacc.Bacc("TRN2", target_bir_lowering=False, num_devices=1)
    arrays, args = {}, []
    given = {n: np.ascontiguousarray(inputs[n]) for n in _INS}
    for name, a in [*given.items(), ("tables", constant_table())]:
        arrays[f"in_{name}_dram"] = a
        args.append(nc.dram_tensor(f"in_{name}_dram", a.shape, mybir.dt.from_np(a.dtype),
                                   kind="ExternalInput").ap())
    args.append(nc.dram_tensor("out_0_dram", (1, SEQ, D), mybir.dt.float32,
                               kind="ExternalOutput").ap())
    build(nc, *args)
    r = _run(nc, [arrays], core_ids=[0])
    return r.results[0]["out_0_dram"]
```
